# Optimizing a Trainium2 kernel written in Bass

```python
import numpy as np
import jax
import jax.numpy as jnp
from jax import lax

D_MODEL = 1024
BATCH = 1
SEQ = 256
DEPTH = 1

NSA_HEADS = 8
NSA_KV_GROUPS = 2
NSA_HEAD_DIM = 64
CMP_STRIDE = 16
CMP_LEN = 2 * CMP_STRIDE
CMP_HIDDEN = 128
SEL_BLOCK = 64
SEL_TOPN = 16
WINDOW = 512
Q_BLOCK = 128
ML_HEADS = 4
ML_HEAD_DIM = 128
ML_CHUNK = 64
CONV_WIDTH = 4
N_EXPERTS = 32
TOP_K = 4
D_EXPERT = 1024
SWIGLU_LIMIT = 7.0
SWIGLU_ALPHA = 1.702
MOE_ROWS = 256
NORM_EPS = 1e-6
NEG_INF = -1e30
FORCE_BONUS = 1e4

NSA_QW = NSA_HEADS * NSA_HEAD_DIM
NSA_KVW = NSA_KV_GROUPS * NSA_HEAD_DIM
ML_W = ML_HEADS * ML_HEAD_DIM
IN_SPLITS = (NSA_QW, 6 * NSA_KVW, 3 * NSA_HEADS, 2 * ML_W, ML_W, 2 * ML_HEADS, ML_W, 2 * D_MODEL)
IN_W = sum(IN_SPLITS)

kernel_name = 'hybrid_nsa_mlstm_moe_block'

def rms_norm(x, g):
    xf = x.astype(jnp.float32)
    y = xf * lax.rsqrt(jnp.mean(xf * xf, axis=-1, keepdims=True) + NORM_EPS)
    return (y * g.astype(jnp.float32)).astype(x.dtype)

def split_cols(t, sizes):
    cuts = [int(v) for v in np.cumsum(sizes)[:-1]]
    return jnp.split(t, cuts, axis=-1)

def causal_conv(x, w, b):
    C = x.shape[-1]
    y = lax.conv_general_dilated(x, w[:, None, :].astype(x.dtype), window_strides=(1,),
                                 padding=((CONV_WIDTH - 1, 0),),
                                 dimension_numbers=('NWC', 'WIO', 'NWC'),
                                 feature_group_count=C)
    return y + b

def nsa_compress(t, pe, w1, w2):
    B, G, S, dh = t.shape
    nc = S // CMP_STRIDE - 1
    t16 = t.reshape(B, G, S // CMP_STRIDE, CMP_STRIDE, dh)
    blocks = jnp.concatenate([t16[:, :, :-1], t16[:, :, 1:]], axis=3) + pe
    return jax.nn.gelu(blocks.reshape(B, G, nc, CMP_LEN * dh) @ w1) @ w2

def nsa_mixer(q, kv, gate_pre, pe_k, pe_v, w1_k, w2_k, w1_v, w2_v):
    B, S, _ = q.shape
    G, R, dh = NSA_KV_GROUPS, NSA_HEADS // NSA_KV_GROUPS, NSA_HEAD_DIM
    scale = dh ** -0.5
    f32 = jnp.float32
    qh = q.reshape(B, S, G, R, dh).transpose(0, 2, 3, 1, 4)
    kvh = kv.reshape(B, S, 6, G, dh).transpose(2, 0, 3, 1, 4)
    k_cmp, v_cmp, k_sel, v_sel, k_win, v_win = kvh[0], kvh[1], kvh[2], kvh[3], kvh[4], kvh[5]
    tpos = jnp.arange(S)

    kc = nsa_compress(k_cmp, pe_k, w1_k, w2_k)
    vc = nsa_compress(v_cmp, pe_v, w1_v, w2_v)
    nc = kc.shape[2]
    cmp_mask = (jnp.arange(nc) * CMP_STRIDE + CMP_LEN - 1)[None, :] <= tpos[:, None]
    s_c = jnp.einsum('bgrsd,bgnd->bgrsn', qh, kc).astype(f32) * scale
    p_c = jax.nn.softmax(jnp.where(cmp_mask, s_c, NEG_INF), axis=-1) * cmp_mask
    o_cmp = jnp.einsum('bgrsn,bgnd->bgrsd', p_c.astype(vc.dtype), vc)

    ns = S // SEL_BLOCK
    n_sel = min(SEL_TOPN, ns)
    c0 = np.arange(nc) * CMP_STRIDE
    s0 = np.arange(ns) * SEL_BLOCK
    overlap = np.clip(np.minimum(c0[:, None] + CMP_LEN, s0[None, :] + SEL_BLOCK)
                      - np.maximum(c0[:, None], s0[None, :]), 0, None) / CMP_LEN
    imp = jnp.einsum('bgsn,nj->bgsj', p_c.sum(axis=2), jnp.asarray(overlap, f32))
    cur = (tpos // SEL_BLOCK)[:, None]
    blk = jnp.arange(ns)[None, :]
    forced = (blk == 0) | (blk == cur) | (blk == cur - 1)
    imp = jnp.where(blk > cur, NEG_INF, imp + FORCE_BONUS * forced)
    _, sel_idx = lax.top_k(imp, n_sel)

    nqb = S // Q_BLOCK
    kb_sel = k_sel.reshape(B, G, ns, SEL_BLOCK, dh)
    vb_sel = v_sel.reshape(B, G, ns, SEL_BLOCK, dh)
    pad = jnp.zeros((B, G, WINDOW, dh), k_win.dtype)
    k_win_p = jnp.concatenate([pad, k_win], axis=2)
    v_win_p = jnp.concatenate([pad, v_win], axis=2)
    q_blocks = qh.reshape(B, G, R, nqb, Q_BLOCK, dh).transpose(3, 0, 1, 2, 4, 5)
    idx_blocks = sel_idx.reshape(B, G, nqb, Q_BLOCK, n_sel).transpose(2, 0, 1, 3, 4)
    gather_blocks = jax.vmap(jax.vmap(lambda blocks, idx: blocks[idx]))
    n_keys = n_sel * SEL_BLOCK

    def block_attn(args):
        qb, ib, bi = args
        tq = bi * Q_BLOCK + jnp.arange(Q_BLOCK)
        ks = gather_blocks(kb_sel, ib).reshape(B, G, Q_BLOCK, n_keys, dh)
        vs = gather_blocks(vb_sel, ib).reshape(B, G, Q_BLOCK, n_keys, dh)
        pos = (ib[..., None] * SEL_BLOCK + jnp.arange(SEL_BLOCK)).reshape(B, G, Q_BLOCK, n_keys)
        smask = (pos <= tq[:, None])[:, :, None]
        s = jnp.einsum('bgrqd,bgqkd->bgrqk', qb, ks).astype(f32) * scale
        p = jax.nn.softmax(jnp.where(smask, s, NEG_INF), axis=-1)
        o_s = jnp.einsum('bgrqk,bgqkd->bgrqd', p.astype(vs.dtype), vs)
        kw = lax.dynamic_slice_in_dim(k_win_p, bi * Q_BLOCK, Q_BLOCK + WINDOW, axis=2)
        vw = lax.dynamic_slice_in_dim(v_win_p, bi * Q_BLOCK, Q_BLOCK + WINDOW, axis=2)
        kpos = bi * Q_BLOCK - WINDOW + jnp.arange(Q_BLOCK + WINDOW)
        rel = tq[:, None] - kpos[None, :]
        wmask = (rel >= 0) & (rel < WINDOW) & (kpos[None, :] >= 0)
        s = jnp.einsum('bgrqd,bgkd->bgrqk', qb, kw).astype(f32) * scale
        p = jax.nn.softmax(jnp.where(wmask, s, NEG_INF), axis=-1)
        o_w = jnp.einsum('bgrqk,bgkd->bgrqd', p.astype(vw.dtype), vw)
        return o_s, o_w

    o_sel, o_win = lax.map(block_attn, (q_blocks, idx_blocks, jnp.arange(nqb)))
    o_sel = o_sel.transpose(1, 2, 3, 0, 4, 5).reshape(B, G, R, S, dh)
    o_win = o_win.transpose(1, 2, 3, 0, 4, 5).reshape(B, G, R, S, dh)

    g = jax.nn.sigmoid(gate_pre.astype(f32)).astype(q.dtype)
    g = g.reshape(B, S, 3, G, R).transpose(2, 0, 3, 4, 1)[..., None]
    o = g[0] * o_cmp + g[1] * o_sel + g[2] * o_win
    return o.transpose(0, 3, 1, 2, 4).reshape(B, S, NSA_QW)

def mlstm_mixer(q, k, v, i_pre, f_pre, o_pre, norm_g):
    B, S, _ = q.shape
    H, d, L = ML_HEADS, ML_HEAD_DIM, ML_CHUNK
    nch = S // L
    f32 = jnp.float32

    def heads(t):
        return t.reshape(B, nch, L, H, d).transpose(1, 0, 3, 2, 4).astype(f32)

    def gates(t):
        return t.reshape(B, nch, L, H).transpose(1, 0, 3, 2).astype(f32)

    qc, kc, vc = heads(q), heads(k) * (d ** -0.5), heads(v)
    li = gates(i_pre)
    bcum = jnp.cumsum(jax.nn.log_sigmoid(gates(f_pre)), axis=-1)
    causal = jnp.tril(jnp.ones((L, L), dtype=bool))

    def step(carry, xs):
        C, n, m = carry
        q_, k_, v_, li_, b_ = xs
        D = b_[..., :, None] - b_[..., None, :] + li_[..., None, :]
        D = jnp.where(causal, D, NEG_INF)
        inter = b_ + m[..., None]
        m_t = jnp.maximum(inter, D.max(axis=-1))
        Dw = jnp.exp(D - m_t[..., None])
        inter_w = jnp.exp(inter - m_t)
        qk = jnp.einsum('bhtd,bhsd->bhts', q_, k_) * Dw
        num = jnp.einsum('bhts,bhsd->bhtd', qk, v_) + inter_w[..., None] * jnp.einsum('bhtd,bhde->bhte', q_, C)
        den = qk.sum(axis=-1) + inter_w * jnp.einsum('bhtd,bhd->bht', q_, n)
        h = num / jnp.maximum(jnp.abs(den), jnp.exp(-m_t))[..., None]
        bL = b_[..., -1]
        a = bL[..., None] - b_ + li_
        m_new = jnp.maximum(bL + m, a.max(axis=-1))
        aw = jnp.exp(a - m_new[..., None])
        decay = jnp.exp(bL + m - m_new)
        C_new = decay[..., None, None] * C + jnp.einsum('bhs,bhsd,bhse->bhde', aw, k_, v_)
        n_new = decay[..., None] * n + jnp.einsum('bhs,bhsd->bhd', aw, k_)
        return (C_new, n_new, m_new), h

    init = (jnp.zeros((B, H, d, d), f32), jnp.zeros((B, H, d), f32), jnp.zeros((B, H), f32))
    _, h = lax.scan(step, init, (qc, kc, vc, li, bcum))
    h = h.transpose(1, 0, 3, 2, 4).reshape(B, S, H, d)
    h = h * lax.rsqrt(jnp.mean(h * h, axis=-1, keepdims=True) + NORM_EPS) * norm_g.reshape(H, d).astype(f32)
    h = h * jax.nn.sigmoid(o_pre.astype(f32)).reshape(B, S, H, d)
    return h.reshape(B, S, ML_W).astype(q.dtype)

def token_mixer(n, w_in, pe_k, pe_v, cw1_k, cw2_k, cw1_v, cw2_v, conv_w, conv_b, gate_b, norm_g,
                w_up_nsa, w_up_ml, w_out):
    proj = n @ w_in
    nsa_q, nsa_kv, nsa_g, ml_qk, ml_v, ml_if, ml_o, merge = split_cols(proj, IN_SPLITS)
    o_nsa = nsa_mixer(nsa_q, nsa_kv, nsa_g, pe_k, pe_v, cw1_k, cw2_k, cw1_v, cw2_v)
    ml_qk = jax.nn.silu(causal_conv(ml_qk, conv_w, conv_b))
    ml_q, ml_k = jnp.split(ml_qk, 2, axis=-1)
    ml_if = ml_if + gate_b
    o_ml = mlstm_mixer(ml_q, ml_k, ml_v, ml_if[..., :ML_HEADS], ml_if[..., ML_HEADS:], ml_o, norm_g)
    g_nsa, g_ml = jnp.split(jax.nn.sigmoid(merge.astype(jnp.float32)).astype(n.dtype), 2, axis=-1)
    return (g_nsa * (o_nsa @ w_up_nsa) + g_ml * (o_ml @ w_up_ml)) @ w_out

def moe_ffn(x, w_router, b_router, w1, b1, w2, b2):
    B, S, D = x.shape
    T = B * S
    A = T * TOP_K
    xt = x.reshape(T, D)
    logits = (xt @ w_router + b_router).astype(jnp.float32)
    top_v, top_i = lax.top_k(logits, TOP_K)
    gate = jax.nn.softmax(top_v, axis=-1)
    e_flat = top_i.reshape(A)
    tok_flat = jnp.arange(A) // TOP_K
    order = jnp.argsort(e_flat)
    e_s, tok_s, g_s = e_flat[order], tok_flat[order], gate.reshape(A)[order]
    counts = jnp.bincount(e_flat, length=N_EXPERTS)
    padded = (counts + MOE_ROWS - 1) // MOE_ROWS * MOE_ROWS
    grp_start = jnp.cumsum(counts) - counts
    pad_end = jnp.cumsum(padded)
    pad_start = pad_end - padded
    dest = pad_start[e_s] + jnp.arange(A) - grp_start[e_s]
    n_blk = -(-(A + N_EXPERTS * (MOE_ROWS - 1)) // MOE_ROWS)
    P = n_blk * MOE_ROWS
    row_tok = jnp.full((P,), T, dtype=jnp.int32).at[dest].set(tok_s.astype(jnp.int32))
    row_gate = jnp.zeros((P,), jnp.float32).at[dest].set(g_s)
    blk_expert = jnp.minimum(jnp.searchsorted(pad_end, jnp.arange(n_blk) * MOE_ROWS, side='right'),
                             N_EXPERTS - 1)
    x_pad = jnp.concatenate([xt, jnp.zeros((1, D), xt.dtype)], axis=0)
    x_rows = x_pad[row_tok].reshape(n_blk, MOE_ROWS, D)

    def expert_block(args):
        xb, e = args
        hcat = xb @ w1[e] + b1[e]
        glu = jnp.minimum(hcat[:, :D_EXPERT], SWIGLU_LIMIT)
        lin = jnp.clip(hcat[:, D_EXPERT:], -SWIGLU_LIMIT, SWIGLU_LIMIT)
        act = glu * jax.nn.sigmoid(SWIGLU_ALPHA * glu) * (lin + 1.0)
        return act @ w2[e] + b2[e]

    y_rows = lax.map(expert_block, (x_rows, blk_expert)).reshape(P, D)
    y_rows = y_rows * row_gate[:, None].astype(y_rows.dtype)
    y = jax.ops.segment_sum(y_rows, row_tok, num_segments=T + 1)[:T]
    return y.reshape(B, S, D)

def setup_inputs(seed: int = 0) -> dict:
    key = jax.random.key(seed)
    ks = jax.random.split(key, 32)
    f32 = jnp.float32

    def nrm(k, shape, scale):
        return jax.random.normal(k, shape, f32) * scale

    dh = NSA_HEAD_DIM
    return {
        'x': nrm(ks[0], (BATCH, SEQ, D_MODEL), 1.0),
        'c': nrm(ks[1], (BATCH, D_MODEL), 1.0),
        'ada_w': nrm(ks[2], (DEPTH, D_MODEL, 6 * D_MODEL), 0.5 * D_MODEL ** -0.5),
        'ada_b': nrm(ks[3], (DEPTH, 6 * D_MODEL), 0.02),
        'norm1_g': 1.0 + nrm(ks[4], (DEPTH, D_MODEL), 0.02),
        'w_in': nrm(ks[5], (DEPTH, D_MODEL, IN_W), D_MODEL ** -0.5),
        'nsa_pe_k': nrm(ks[6], (DEPTH, CMP_LEN, dh), 0.02),
        'nsa_pe_v': nrm(ks[7], (DEPTH, CMP_LEN, dh), 0.02),
        'nsa_cmp_w1_k': nrm(ks[8], (DEPTH, CMP_LEN * dh, CMP_HIDDEN), (CMP_LEN * dh) ** -0.5),
        'nsa_cmp_w2_k': nrm(ks[9], (DEPTH, CMP_HIDDEN, dh), CMP_HIDDEN ** -0.5),
        'nsa_cmp_w1_v': nrm(ks[10], (DEPTH, CMP_LEN * dh, CMP_HIDDEN), (CMP_LEN * dh) ** -0.5),
        'nsa_cmp_w2_v': nrm(ks[11], (DEPTH, CMP_HIDDEN, dh), CMP_HIDDEN ** -0.5),
        'ml_conv_w': nrm(ks[12], (DEPTH, CONV_WIDTH, 2 * ML_W), CONV_WIDTH ** -0.5),
        'ml_conv_b': nrm(ks[13], (DEPTH, 2 * ML_W), 0.02),
        'ml_gate_b': jnp.concatenate([nrm(ks[14], (DEPTH, ML_HEADS), 0.1),
                                      3.0 + nrm(ks[15], (DEPTH, ML_HEADS), 0.5)], axis=-1),
        'ml_norm_g': 1.0 + nrm(ks[16], (DEPTH, ML_W), 0.02),
        'w_up_nsa': nrm(ks[17], (DEPTH, NSA_QW, D_MODEL), NSA_QW ** -0.5),
        'w_up_ml': nrm(ks[18], (DEPTH, ML_W, D_MODEL), ML_W ** -0.5),
        'w_out': nrm(ks[19], (DEPTH, D_MODEL, D_MODEL), D_MODEL ** -0.5),
        'norm2_g': 1.0 + nrm(ks[20], (DEPTH, D_MODEL), 0.02),
        'router_w': nrm(ks[21], (DEPTH, D_MODEL, N_EXPERTS), D_MODEL ** -0.5),
        'router_b': nrm(ks[22], (DEPTH, N_EXPERTS), 0.01),
        'exp_w1': nrm(ks[23], (DEPTH, N_EXPERTS, D_MODEL, 2 * D_EXPERT), D_MODEL ** -0.5),
        'exp_b1': nrm(ks[24], (DEPTH, N_EXPERTS, 2 * D_EXPERT), 0.02),
        'exp_w2': nrm(ks[25], (DEPTH, N_EXPERTS, D_EXPERT, D_MODEL), D_EXPERT ** -0.5),
        'exp_b2': nrm(ks[26], (DEPTH, N_EXPERTS, D_MODEL), 0.02),
        'final_g': 1.0 + nrm(ks[27], (D_MODEL,), 0.02),
    }

def reference(x, c, ada_w, ada_b, norm1_g, w_in, nsa_pe_k, nsa_pe_v, nsa_cmp_w1_k, nsa_cmp_w2_k,
              nsa_cmp_w1_v, nsa_cmp_w2_v, ml_conv_w, ml_conv_b, ml_gate_b, ml_norm_g, w_up_nsa, w_up_ml,
              w_out, norm2_g, router_w, router_b, exp_w1, exp_b1, exp_w2, exp_b2, final_g):
    h = x
    c_act = jax.nn.silu(c)
    for layer in range(DEPTH):
        mod = (c_act @ ada_w[layer] + ada_b[layer])[:, None, :]
        sh1, sc1, gt1, sh2, sc2, gt2 = jnp.split(mod, 6, axis=-1)
        n = rms_norm(h, norm1_g[layer]) * (1.0 + sc1) + sh1
        mix = token_mixer(n, w_in[layer], nsa_pe_k[layer], nsa_pe_v[layer], nsa_cmp_w1_k[layer],
                          nsa_cmp_w2_k[layer], nsa_cmp_w1_v[layer], nsa_cmp_w2_v[layer], ml_conv_w[layer],
                          ml_conv_b[layer], ml_gate_b[layer], ml_norm_g[layer], w_up_nsa[layer],
                          w_up_ml[layer], w_out[layer])
        h = h + (1.0 + gt1) * mix
        n = rms_norm(h, norm2_g[layer]) * (1.0 + sc2) + sh2
        h = h + (1.0 + gt2) * moe_ffn(n, router_w[layer], router_b[layer], exp_w1[layer], exp_b1[layer],
                                      exp_w2[layer], exp_b2[layer])
    return rms_norm(h, final_g)


_drawn_inputs = setup_inputs


def setup_inputs(seed=0):
    import zlib

    import numpy as np

    out = dict(_drawn_inputs(seed))
    spreads = {}
    factors = {'nsa_pe_k': 8.0,
     'nsa_pe_v': 7.604,
     'ml_conv_b': 4.508,
     'exp_b1': 4.997,
     'exp_b2': 6.052,
     'final_g': 3.134}
    for name, (base, spread) in spreads.items():
        noise = np.random.default_rng([zlib.crc32(name.encode()), seed]).standard_normal(out[name].shape)
        drawn = base * np.exp(spread * noise) if base else spread * noise
        out[name] = jnp.asarray(drawn.astype(out[name].dtype))
    for name, factor in factors.items():
        out[name] = (out[name] * factor).astype(out[name].dtype)
    return out
```

```python
from contextlib import ExitStack

import concourse.bass as bass
from concourse import mybir

ALU = mybir.AluOpType
ACT = mybir.ActivationFunctionType
F32 = mybir.dt.float32
BF16 = mybir.dt.bfloat16
I32 = mybir.dt.int32
U32 = mybir.dt.uint32
AX = mybir.AxisListType.X

P = 128


def hybrid_block(nc, x, c, ada_w, ada_b, norm1_g, w_in, pe_k, pe_v, cw1_k, cw2_k, cw1_v, cw2_v,
                 conv_w, conv_b, gate_b, norm_g, w_up_nsa, w_up_ml, w_out, norm2_g,
                 router_w, router_b, exp_w1, exp_b1, exp_w2, exp_b2, final_g, out):
    T, D = x.shape
    TT, KD = T // P, D // P
    HD = D // 2
    NH, DH = 8, 64
    NR = NH // 2
    MH = 4
    EPS = 1e-6
    NSA_SCALE = DH ** -0.5
    ML_SCALE = P ** -0.5
    STRIDE, CLEN = 16, 32
    NCMP = T // STRIDE - 1
    NG = 2 * NCMP
    LT = CLEN * DH // P
    NE = router_w.shape[1]
    TOPK = 4
    SLOTS = 64
    NBLK = T // SLOTS
    LIMIT, ALPHA = 7.0, 1.702
    GELU_A, GELU_B = 2.0 * (2.0 / 3.141592653589793) ** 0.5, 0.044715

    C_Q, C_KV, C_NG = 0, 512, 1280
    C_QK, C_V, C_IF, C_O, C_MG = 1304, 2328, 2840, 2848, 3360

    RING, RW = 12, 2048
    MASKS, SMALL = 10, 16 * 11

    sched = [("small",), ("norm", 0)]
    sched += [("ada", 0, k) for k in range(KD)] + [("mod", 0), ("rows1",), ("turn", 0), ("params",)]
    sched += [("proj", C_KV), ("proj", C_KV + 256), ("proj", C_KV + 512), ("proj", C_Q), ("proj", C_Q + 256), ("gates",)]
    ada_left = [("ada", p, k) for p in (1, 2) for k in range(KD)]
    wide = [C_QK + 256 * i for i in range(4)] + [C_V, C_V + 256, C_O, C_O + 256]
    wide += [C_MG + 256 * i for i in range(8)]
    for i, col in enumerate(wide):
        sched.append(("proj", col))
        if i < 4:
            sched.append(("conv", i))
        if i == 0:
            sched += [("compress", 0), ("compress", 1)]
        if i == 1:
            sched += [("gate_cols",), ("cmp_keys",)]
        if i == 2:
            sched.append(("cmp_scores",))
        if i < 4:
            sched.append(("conv_act", i))
        if 0 <= i - 5 < NH:
            sched.append(("head_out", i - 5))
        if 0 <= i - 12 < MH:
            sched.append(("ml_out", i - 12))
        if 0 <= i - 4 < NH:
            sched.append(("head_turn", i - 4))
        if 0 <= i - 3 < NH:
            sched.append(("head_scores", i - 3))
        if 0 <= i - 11 < MH:
            sched.append(("ml_scores", i - 11))
        sched.append(ada_left.pop(0))
        if i == 7 or i == 15:
            sched.append(("mod", i // 8 + 1))
    sched += [("ml_norm",), ("up", 0), ("ml_turn",), ("up", 1), ("rows2", 0)]
    sched += [("mix", 0), ("rows2", 1)] + [("mix", i) for i in range(1, KD // 2)]
    sched += [("add_mix",), ("norm", 1), ("turn", 1), ("router",)]

    STREAMED = {"ada": 1, "proj": 1, "compress": 1, "up": 2, "mix": 1}
    loads, order, at_, per_slot = {}, [], 0, [0] * RING
    for item in sched:
        n = STREAMED.get(item[0], 0)
        if n:
            at_ += at_ % RING + n > RING
            s = at_ % RING
            per_slot[s] += 64 if item[0] == "proj" and item[1] < C_KV else 16
            loads[item] = (s, n, at_, per_slot[s])
            order.append(item)
            at_ += n
    MOE0 = at_
    PER_E = KD + KD // 2
    assert PER_E == RING

    with ExitStack() as ctx:
        def sb(name, shape, dt=F32):
            return ctx.enter_context(nc.sbuf_tensor(name, shape, dt))

        def psum(name):
            return ctx.enter_context(nc.psum_tensor(name, [P, 512], F32))

        def sem(name):
            return ctx.enter_context(nc.semaphore(name))

        ring = sb("ring", [P, RING, RW])
        xres = sb("xres", [P, TT, D])
        ntok = sb("ntok", [P, TT, D])
        nT = sb("nT", [P, KD, T])
        ident = sb("ident", [P, P])
        identb = sb("identb", [P, P], BF16)
        cmaskb = sb("cmaskb", [P, P], BF16)
        tmaskb = sb("tmaskb", [P, P], BF16)
        sel0 = sb("sel0", [P, P])
        sel4 = sb("sel4", [MH, MH, P])
        ones = sb("ones", [P, P])
        lower = sb("lower", [P, P])
        modrow = sb("modrow", [P, 3, 512])
        small = sb("small", [P, 256])
        crep = sb("crep", [P, KD, 32])
        wgate = sb("wgate", [P, KD, 32])
        wr = sb("wr", [P, KD, NE])

        ARENA = 18412
        arena = sb("arena", [P, ARENA])
        used = {"f": 0, "m": 0}

        def view(side, n, parts=P):
            o = used[side]
            used[side] += n
            assert used[side] <= ARENA, (side, used[side])
            return arena[0:parts, o:o + n]

        sg = view("f", 16 * T).rearrange("p (m t) -> p m t", m=16)
        rowA = view("f", 2 * D).rearrange("p (a d) -> p a d", a=2)
        mlc = rowA.rearrange("p a d -> p (a d)").rearrange("p (m t) -> p m t", m=8)
        mlx = sg.rearrange("p m t -> p (m t)")[:, 0:8 * (T + 3)].rearrange("p (m t) -> p m t", m=8)
        qT = view("f", NR * T).rearrange("p (r t) -> p r t", r=NR)
        kT = view("f", 2 * T).rearrange("p (b t) -> p b t", b=2)
        vS = view("f", TT * 2 * P).rearrange("p (s b e) -> p s b e", s=TT, b=2)
        mlv = view("f", TT * MH * 129).rearrange("p (s h e) -> p s h e", s=TT, h=MH)
        mlo = view("f", TT * 512).rearrange("p (s e) -> p s e", s=TT)
        Pb = view("f", 2 * TT * 2 * T).rearrange("p (z s b t) -> p z s b t", z=2, s=TT, b=2)
        kpe = Pb.rearrange("p z s b t -> p (z s b t)")[:, 0:2 * LT * NG].rearrange(
            "p (v i n) -> p v i n", v=2, i=LT)
        PTb = view("f", 2 * 384).rearrange("p (b t) -> p b t", b=2)
        MPT = view("f", 384)
        PcT = view("f", 256)
        Pc = view("f", TT * NH * NCMP).rearrange("p (s h n) -> p s h n", s=TT, h=NH)
        Zc = view("f", TT * NH * NCMP).rearrange("p (s h n) -> p s h n", s=TT, h=NH)
        cneg = view("f", TT * NH * NCMP).rearrange("p (s h n) -> p s h n", s=TT, h=NH)
        c01 = view("f", TT * NH * NCMP).rearrange("p (s h n) -> p s h n", s=TT, h=NH)
        oT = view("f", 4 * T).rearrange("p (j t) -> p j t", j=4)
        grow_all = view("f", 8 * T)
        grow = grow_all.rearrange("p (m t) -> p m t", m=8)[0:MH]
        mlT = grow_all[:, 0:4 * T].rearrange("p (j t) -> p j t", j=4)
        hml = ntok[:, 0, :].rearrange("p (s e) -> p s e", s=TT)
        hsq = ntok[:, 1, :].rearrange("p (s e) -> p s e", s=TT)
        cw2 = view("f", 2 * DH).rearrange("p (v e) -> p v e", v=2)
        cw2d = view("f", P)
        hid = view("f", 2 * NG).rearrange("p (v n) -> p v n", v=2)
        htmp = view("f", 2 * NG).rearrange("p (v n) -> p v n", v=2)
        kcT = view("f", NG)
        vc = view("f", 2 * DH).rearrange("p (g e) -> p g e", g=2)
        peT = view("f", 2 * LT).rearrange("p (v i) -> p v i", v=2)
        gcol = view("f", 16).rearrange("p (a s h) -> p a s h", a=2, s=TT)
        convw = view("f", 4 * 8).rearrange("p (w m) -> p w m", w=4)
        convb = view("f", 8)
        ngc = view("f", MH)
        gb = view("f", 2)
        gn = view("f", TT * 24).rearrange("p (s n) -> p s n", s=TT)
        raw = Pb.rearrange("p z s b t -> p (z s b t)")[:, 2 * LT * NG:]
        peraw = raw[:, 0:2 * P].rearrange("p (v e) -> p v e", v=2)
        cwraw = raw[:, 2 * P:4 * P]
        craw = raw[:, 4 * P:5 * P]
        ngraw = raw[:, 5 * P:6 * P]
        merged = mlc
        mtmp = Pb[:, 0].rearrange("p s b t -> p (s b t)")[:, 0:512]

        rg1 = view("m", D)
        rs2 = view("m", D)
        rsh2 = view("m", D)
        rg2 = view("m", D)
        used["m"] = 16 * T + 2 * D
        rfin = view("m", D)
        ob = view("m", TT * D)
        b1all = ob[0:NE, :]
        otmp = ob.rearrange("p (s d) -> p s d", s=TT)
        b2all = view("m", D, NE)
        onehot = view("m", TT * SLOTS).rearrange("p (s n) -> p s n", s=TT)
        onegate = view("m", TT * P).rearrange("p (s n) -> p s n", s=TT)
        sel_e = view("m", SLOTS, NE)
        xg = view("m", 512)
        xgT = view("m", 512).rearrange("p (m h s) -> p m h s", m=4, h=2)
        glu = view("m", 512)
        lin = view("m", 512)
        sgm = view("m", 512)
        act_t = view("m", 512)
        actT = view("m", 512).rearrange("p (m h s) -> p m h s", m=4, h=2)
        ysb = view("m", 512)
        GT = view("m", T)
        gatesT = view("m", T, NE)
        rank = view("m", TT * (NE + 1)).rearrange("p (s e) -> p s e", s=TT)
        gate = view("m", TT * NE).rearrange("p (s e) -> p s e", s=TT)
        memb = view("m", TT * NE).rearrange("p (s e) -> p s e", s=TT)
        logit = view("m", TT * NE).rearrange("p (s e) -> p s e", s=TT)
        wtmp = view("m", NE)
        rbias = view("m", NE)

        iota_f = view("m", NBLK * 2 * SLOTS).rearrange("p (b a n) -> p b a n", b=NBLK, a=2)
        top8 = sb("top8", [P, TT, 8])
        idx8 = sb("idx8", [P, TT, 8], U32)
        idxf = sb("idxf", [P, TT, 8])
        cntf = view("m", 4 * NE, 1).rearrange("p (a e) -> p a e", a=4)
        cnt_t = sb("cnt_t", [1, NE], I32)
        next_t = sb("next_t", [1, NBLK, NE + 1], I32)
        blk_t = sb("blk_t", [1, NE + 1], I32)

        at = [0]

        def piece(n):
            at[0] += n
            return small[:, at[0] - n:at[0]]

        sqj = nT[:, :, :].rearrange("p k t -> p (k t)").rearrange("p (s d) -> p s d", s=TT)
        ssq, std, rstd = piece(TT), piece(TT), piece(TT)
        ccol, csig = piece(KD), piece(KD)
        mx = piece(NH * 4).rearrange("p (h s b) -> p h s b", h=NH, s=TT)
        nmx = piece(NH * 4).rearrange("p (h s b) -> p h s b", h=NH, s=TT)
        psum_p = piece(NH * 4).rearrange("p (h s b) -> p h s b", h=NH, s=TT)
        rsc = piece(NH * 4).rearrange("p (h s b) -> p h s b", h=NH, s=TT)
        cmx = piece(TT * NH).rearrange("p (s h) -> p s h", s=TT)
        csum = piece(TT * NH).rearrange("p (s h) -> p s h", s=TT)
        den = piece(MH * TT).rearrange("p (h s) -> p h s", h=MH)
        hss = piece(TT * MH)
        hstd = piece(TT * MH)
        hr = piece(TT * MH)
        gsum = piece(TT)
        grs = piece(TT)
        gexp = piece(TT * TOPK).rearrange("p (s j) -> p s j", s=TT)
        nmax = piece(TT)

        PJ = [psum("PJ0"), psum("PJ1")]
        SC = [psum("SC0"), psum("SC1")]
        PT = [psum("PT0"), psum("PT1")]
        OB = [psum("OB0"), psum("OB1")]
        ACC = [[PT[0], PT[1]], [OB[0], OB[1]]]
        HG, HL = SC
        XB, YB = PJ

        arrived = [sem(f"arrived{i}") for i in range(RING)]
        ring_free = sem("ring_free")
        ada_chunk = sem("ada_chunk")
        mix_chunk = sem("mix_chunk")
        x_in = sem("x_in")
        small_in = sem("small_in")
        c_in = sem("c_in")
        turned_c = sem("turned_c")
        params_done = sem("params_done")
        gains_in = sem("gains_in")
        adab_in = sem("adab_in")
        moe_in = sem("moe_in")
        rfin_in = sem("rfin_in")
        consts = sem("consts")
        masks = sem("masks")
        iota_made = sem("iota_made")
        pool_chain = sem("pool_chain")
        dve_chain = sem("dve_chain")
        act_chain = sem("act_chain")
        ssq_done = [sem("ssq1"), sem("ssq2"), sem("ssq3")]
        var_done = [sem("var1"), sem("var2"), sem("var3"), sem("var_ml")]
        std_done = [sem("std1"), sem("std2"), sem("std3"), sem("std_ml")]
        turned_small = sem("turned_small")
        small_copied = sem("small_copied")
        c_exp = sem("c_exp")
        crep_done = sem("crep_done")
        mod_done = sem("mod_done")
        rows_done = sem("rows_done")
        rows_used = sem("rows_used")
        rows_used_act = sem("rows_used_act")
        ntok_done = sem("ntok_done")
        n_turned = sem("n_turned")
        nT_copied = [sem("nT_copied0"), sem("nT_copied1")]
        proj_done = sem("proj_done")
        proj_taken = [sem("proj_taken0"), sem("proj_taken1")]
        gates_done = sem("gates_done")
        gexp_done = sem("gexp_done")
        ls_exp = sem("ls_exp")
        ls_in = sem("ls_in")
        ls_ln = sem("ls_ln")
        nm_in = sem("nm_in")
        grow_done = sem("grow_done")
        gcol_turned = sem("gcol_turned")
        gcol_done = sem("gcol_done")
        kpe_done = sem("kpe_done")
        hid_done = sem("hid_done")
        gelu_in = sem("gelu_in")
        gelu_exp = sem("gelu_exp")
        hid_act = sem("hid_act")
        cmp_kv = sem("cmp_kv")
        cmp_kv_sb = sem("cmp_kv_sb")
        cmp_score = sem("cmp_score")
        cmp_sub = sem("cmp_sub")
        cmp_exp = sem("cmp_exp")
        cmp_p = sem("cmp_p")
        score_done = sem("score_done")
        max_done = sem("max_done")
        exp_done = sem("exp_done")
        probs_done = sem("probs_done")
        pt_done = sem("pt_done")
        pt_copied = [sem("pt_copied0"), sem("pt_copied1")]
        o_done = sem("o_done")
        o_copied = sem("o_copied")
        mls_done = sem("mls_done")
        mle_done = sem("mle_done")
        mpt_done = sem("mpt_done")
        num_done = sem("num_done")
        hml_done = sem("hml_done")
        hml_norm = sem("hml_norm")
        conv_done = sem("conv_done")
        conv_exp = sem("conv_exp")
        conv_act = sem("conv_act")
        mlT_turned = sem("mlT_turned")
        mlT_copied = sem("mlT_copied")
        sig_done = sem("sig_done")
        up_done = sem("up_done")
        up_taken = sem("up_taken")
        merged_done = sem("merged_done")
        mix_done = sem("mix_done")
        mix_taken = sem("mix_taken")
        h_done = sem("h_done")
        router_done = sem("router_done")
        top_done = sem("top_done")
        top_exp = sem("top_exp")
        memb_done = sem("memb_done")
        rank_psum = sem("rank_psum")
        table_done = sem("table_done")
        gatesT_psum = sem("gatesT_psum")
        gatesT_done = sem("gatesT_done")
        hot_done = sem("hot_done")
        onegate_done = sem("onegate_done")
        gathered = sem("gathered")
        xg_copied = sem("xg_copied")
        xg_turned = sem("xg_turned")
        xgT_copied = sem("xgT_copied")
        gt_turned = sem("gt_turned")
        gt_copied = sem("gt_copied")
        biased = sem("biased")
        h_psum = sem("h_psum")
        glu_min = sem("glu_min")
        sig_glu = sem("sig_glu")
        glu_gated = sem("glu_gated")
        act_made = sem("act_made")
        act_turned = sem("act_turned")
        actT_copied = sem("actT_copied")
        y_psum = sem("y_psum")
        y_copied = sem("y_copied")
        added = sem("added")
        final_done = sem("final_done")
        out_done = sem("out_done")

        block = ctx.enter_context(nc.Block())

        freed, n_proj, n_ada = {}, 0, 0
        for item in order:
            if item[0] == "proj":
                n_proj += 1
                freed[item] = (proj_done, n_proj)
            elif item[0] == "ada":
                n_ada += 1
                freed[item] = (ada_chunk, n_ada)
            elif item[0] == "compress":
                freed[item] = (hid_done, item[1] + 1)
            elif item[0] == "up":
                freed[item] = (up_done, 4 * (item[1] + 1))
            else:
                freed[item] = (mix_chunk, item[1] + 1)
        owner = {}
        for item in order:
            s, n, at_, _ = loads[item]
            for a in range(n):
                owner[at_ + a] = item

        def owners_before(at_, n):
            found = []
            for a in range(at_, at_ + n):
                back = a - RING
                while back >= 0 and back not in owner:
                    back -= RING
                if back >= 0 and freed[owner[back]] not in found:
                    found.append(freed[owner[back]])
            return found

        def arrive(eng, item):
            s, _, _, count = loads[item]
            eng.wait_ge(arrived[s], count)

        def ring_k(item):
            return ring[:, loads[item][0], :].rearrange("p (k n) -> p k n", k=KD)

        def each_block(eng, body):
            with eng.Fori(0, NE) as e:
                cnt = eng.value_load(cnt_t[0:1, bass.ds(e, 1)], min_val=0, max_val=T)
                before = eng.value_load(blk_t[0:1, bass.ds(e, 1)], min_val=0, max_val=NBLK * NE)
                num = eng.value_load(blk_t[0:1, bass.ds(e + 1, 1)], min_val=1, max_val=NBLK * NE)
                for b in range(1, NBLK):
                    with eng.If(cnt > SLOTS * b):
                        body(e, before + b, b, False)
                body(e, num, 0, True)

        @block.sync
        def _(sp):
            def expert_chunk(e, ch):
                s = (MOE0 + ch) % RING
                if ch < KD:
                    src = exp_w1[bass.ds(e, 1), ch * P:(ch + 1) * P, :].rearrange("a p n -> p a n")
                    dst = ring[:, s, :].rearrange("p (a n) -> p a n", a=1)
                else:
                    r0 = (ch - KD) * 2 * P
                    src = exp_w2[bass.ds(e, 1), r0:r0 + 2 * P, :].rearrange("a (k p) n -> p (a k) n", p=P)
                    dst = ring[:, s, :].rearrange("p (k n) -> p k n", n=D)
                sp.dma_start(dst, src).then_inc(arrived[s], 16)

            sp.dma_start(craw[0:KD, :], c.rearrange("a (k p) -> (a k) p", p=P)).then_inc(c_in, 16)
            sp.dma_start(xres[:], x.rearrange("(s p) d -> p s d", p=P)).then_inc(x_in, 16)
            for item in order:
                kind = item[0]
                s, n, at_, _ = loads[item]
                for event, value in owners_before(at_, n):
                    sp.wait_ge(event, value)
                if kind == "ada":
                    _, p, k = item
                    sp.dma_start(ring[:, s, :], ada_w[k * P:(k + 1) * P, p * RW:(p + 1) * RW]).then_inc(arrived[s], 16)
                elif kind == "proj" and item[1] < C_KV:
                    dst = ring_k(item).rearrange("p k (r g d) -> p k r g d", r=2, g=2)
                    for r in range(2):
                        for g in range(2):
                            a = item[1] // 2 + (g * NR + r) * DH
                            sp.dma_start(dst[:, :, r, g, :], w_in[:, a:a + DH].rearrange("(k p) n -> p k n", p=P)
                                         ).then_inc(arrived[s], 16)
                elif kind == "proj":
                    sp.dma_start(ring_k(item), w_in[:, item[1]:item[1] + 256].rearrange("(k p) n -> p k n", p=P)
                                 ).then_inc(arrived[s], 16)
                elif kind == "compress":
                    sp.dma_start(ring[:, s, :].rearrange("p (i n) -> p i n", i=LT),
                                 (cw1_k, cw1_v)[item[1]].rearrange("(i p) n -> p i n", p=P)).then_inc(arrived[s], 16)
                elif kind == "up":
                    sp.dma_start(ring[:, s:s + 2, :].rearrange("p a (k n) -> p (a k) n", n=D),
                                 (w_up_nsa, w_up_ml)[item[1]].rearrange("(k p) n -> p k n", p=P)).then_inc(arrived[s], 16)
                else:
                    i = item[1]
                    sp.dma_start(ring[:, s, :].rearrange("p (k n) -> p k n", n=D),
                                 w_out[2 * i * P:2 * (i + 1) * P, :].rearrange("(k p) n -> p k n", p=P)
                                 ).then_inc(arrived[s], 16)
            for ch in range(PER_E):
                for event, value in owners_before(MOE0 + ch, 1):
                    sp.wait_ge(event, value)
                expert_chunk(0, ch)
            sp.wait_ge(table_done, 1)
            with sp.Fori(1, NE) as e:
                prev = sp.value_load(blk_t[0:1, bass.ds(e, 1)], min_val=1, max_val=NBLK * NE)
                for ch in range(PER_E):
                    if ch == KD - 1:
                        sp.wait_ge(h_psum, prev)
                    elif ch == PER_E - 1:
                        sp.wait_ge(y_psum, prev)
                    else:
                        sp.wait_ge(ring_free, e * (PER_E - 2) + ((ch if ch >= KD else ch + 1) - (PER_E - 2)))
                    expert_chunk(e, ch)
            sp.wait_ge(final_done, TT)
            sp.dma_start(out.rearrange("(s p) d -> p s d", p=P), otmp).then_inc(out_done, 16)
            sp.wait_ge(out_done, 16)

        @block.gpsimd
        def _(pool):
            chain = [0]

            def link(ins):
                chain[0] += 1
                ins.then_inc(pool_chain, 1)
                pool.wait_ge(pool_chain, chain[0])

            made = {}

            def step(ins, signal):
                made[signal.name] = made.get(signal.name, 0) + 1
                ins.then_inc(signal, 1)
                pool.wait_ge(signal, made[signal.name])

            for v, pe_ in enumerate((pe_k, pe_v)):
                pool.dma_start(peraw[0:LT, v, :], pe_.rearrange("(i a) e -> i (a e)", a=2)).then_inc(small_in, 16)
            pool.dma_start(cwraw[0:32, 0:P], conv_w.rearrange("w (m p) -> (w m) p", p=P)).then_inc(small_in, 16)
            pool.dma_start(cwraw[0:8, P:2 * P], conv_b.rearrange("(m p) -> m p", p=P)).then_inc(small_in, 16)
            pool.dma_start(ngraw[0:MH, :], norm_g.rearrange("(h p) -> h p", p=P)).then_inc(small_in, 16)
            with nc.allow_non_contiguous_dma(reason="eight words"):
                pool.dma_start(gb[0:MH, :], gate_b.rearrange("(a h) -> h a", a=2)).then_inc(small_in, 16)
            for v, w2_ in enumerate((cw2_k, cw2_v)):
                pool.dma_start(cw2[:, v, :], w2_).then_inc(small_in, 16)
            with nc.allow_non_contiguous_dma(reason="gate columns"):
                pool.dma_start(wgate[:, :, 0:24], w_in[:, C_NG:C_NG + 24].rearrange("(k p) n -> p k n", p=P)).then_inc(small_in, 16)
                pool.dma_start(wgate[:, :, 24:32], w_in[:, C_IF:C_IF + 8].rearrange("(k p) n -> p k n", p=P)).then_inc(small_in, 16)
                pool.dma_start(wr[:], router_w.rearrange("(k p) n -> p k n", p=P)).then_inc(small_in, 16)

            link(pool.memset(ident[:], 0.0))
            link(pool.affine_select(out=ident[:], in_=ident[:], compare_op=ALU.not_equal, fill=1.0,
                                    base=0, pattern=[[-1, P]], channel_multiplier=1))
            step(pool.tensor_copy(identb[:], ident[:]), consts)
            link(pool.memset(sel0[:], 0.0))
            for j in range(4):
                ins = pool.memset(sel0[32 * j:32 * j + 1, :], 1.0)
                if j < 3:
                    link(ins)
            step(ins, consts)
            step(pool.memset(ones[:], 1.0), consts)
            link(pool.memset(cmaskb[:], 0.0))
            step(pool.affine_select(out=cmaskb[:], in_=cmaskb[:], compare_op=ALU.is_ge, fill=-1e30,
                               base=0, pattern=[[-1, P]], channel_multiplier=1), masks)
            link(pool.memset(tmaskb[:], 0.0))
            step(pool.affine_select(out=tmaskb[:], in_=tmaskb[:], compare_op=ALU.is_ge, fill=1e30,
                               base=0, pattern=[[1, P]], channel_multiplier=-1), masks)
            link(pool.memset(lower[:], 1.0))
            step(pool.affine_select(out=lower[:], in_=lower[:], compare_op=ALU.is_gt, fill=0.0,
                               base=0, pattern=[[1, P]], channel_multiplier=-1), masks)
            link(pool.memset(sel4[:], 1.0))
            step(pool.affine_select(out=sel4[:], in_=sel4[:], compare_op=ALU.is_equal, fill=0.0,
                               base=0, pattern=[[1, MH], [0, P]], channel_multiplier=-1), masks)
            link(pool.memset(cneg, 0.0))
            link(pool.memset(c01, 1.0))
            for m, f in ((cneg, -1e30), (c01, 0.0)):
                for s in range(TT):
                    step(pool.affine_select(out=m[:, s], in_=m[:, s], compare_op=ALU.is_ge, fill=f,
                                       base=s * P - (CLEN - 1), pattern=[[0, NH], [-STRIDE, NCMP]],
                                       channel_multiplier=1), masks)
            step(pool.memset(mlx[:, :, 0:3], 0.0), masks)
            step(pool.memset(mlv[:, :, :, 128:129], 1.0), masks)
            pool.wait_ge(merged_done, 1)
            pool.iota(iota_f, pattern=[[SLOTS, NBLK], [0, 2], [1, SLOTS]], base=0, channel_multiplier=0,
                      allow_small_or_imprecise_dtypes=True).then_inc(iota_made, 1)
            pool.dma_start(rfin, final_g.rearrange("(a d) -> a d", a=1).to_broadcast([P, D])).then_inc(rfin_in, 16)
            pool.dma_start(b1all, exp_b1).then_inc(moe_in, 16)
            pool.dma_start(b2all, exp_b2).then_inc(moe_in, 16)
            pool.dma_start(rbias, router_b.rearrange("(a d) -> a d", a=1).to_broadcast([P, NE])).then_inc(moe_in, 16)
            pool.dma_start(rg2, norm2_g.rearrange("(a d) -> a d", a=1).to_broadcast([P, D])).then_inc(moe_in, 16)
        @block.tensor
        def _(pe):
            mm, tr = pe.matmul, pe.transpose
            state = {"proj": 0}

            def proj_bank():
                b, n = state["proj"] % 2, state["proj"] // 2
                if n:
                    pe.wait_ge(proj_taken[b], n)
                state["proj"] += 1
                return PJ[b]

            def t_tile(bank, col, w, n0):
                for k in range(KD):
                    last = mm(bank[:, col:col + T], w[:, k, n0:n0 + P], nT[:, k, :],
                              start=(k == 0), stop=(k == KD - 1), skip_group_check=True)
                return last

            def tok_tile(bank, col, w, n0, n, s):
                for k in range(KD):
                    last = mm(bank[:, col:col + n], nT[:, k, s * P:(s + 1) * P], w[:, k, n0:n0 + n],
                              start=(k == 0), stop=(k == KD - 1), skip_group_check=True)
                return last

            def project(item):
                arrive(pe, item)
                bank, w, col = proj_bank(), ring_k(item), item[1]
                if col in (C_KV + 256, C_KV + 512):
                    t_tile(bank, 0, w, 0)
                    tok_tile(bank, T, w, P, P, 0)
                    last = tok_tile(bank, T + P, w, P, P, 1)
                elif C_V <= col < C_MG:
                    tok_tile(bank, 0, w, 0, T, 0)
                    last = tok_tile(bank, T, w, 0, T, 1)
                else:
                    t_tile(bank, 0, w, 0)
                    last = t_tile(bank, T, w, P)
                last.then_inc(proj_done, 1)

            def small_rows():
                pe.wait_ge(consts, 3)
                pe.wait_ge(c_in, 16)
                tr(SC[0][:, 0:KD], craw[0:KD, :], ident[0:KD, 0:KD]).then_inc(turned_c, 1)

            def params():
                pe.wait_ge(small_in, SMALL)
                for v in range(2):
                    tr(OB[1][:, 16 + LT * v:16 + LT * (v + 1)], peraw[0:LT, v, :], ident[0:LT, 0:LT])
                tr(OB[1][:, 64:96], cwraw[0:32, 0:P], ident[0:32, 0:32])
                tr(OB[1][:, 96:104], cwraw[0:8, P:2 * P], ident[0:8, 0:8])
                tr(OB[1][:, 104:108], ngraw[0:MH, :], ident[0:MH, 0:MH]).then_inc(turned_small, 1)

            def ada(item):
                _, p, k = item
                if p == 0 and k == 0:
                    pe.wait_ge(crep_done, 1)
                if p == 1 and k == 0:
                    pe.wait_ge(params_done, 1)
                if p == 2 and k == 0:
                    pe.wait_ge(mod_done, 2)
                arrive(pe, item)
                bank = OB[min(p, 1)]
                for j in range(4):
                    last = mm(bank[32 * j:32 * j + 32, :], crep[:, k, :],
                              ring[:, loads[item][0], j * 512:(j + 1) * 512],
                              start=(k == 0), stop=(k == KD - 1), tile_position=(0, 32 * j), skip_group_check=True)
                last.then_inc(ada_chunk, 1)

            def spread(bank, p, j):
                return mm(bank[:, :], sel0[32 * j:32 * j + 32, :], modrow[32 * j:32 * j + 32, p, :],
                          start=True, stop=True, tile_position=(32 * j, 0))

            def turn_n(base):
                for q in range(4):
                    if q % 2 == 0:
                        pe.wait_ge(ntok_done, 2 * base + q // 2 + 1)
                    if base or q >= 2:
                        pe.wait_ge(nT_copied[q % 2], 2 * base + q // 2)
                    for a in range(2):
                        for s in range(TT):
                            k = 2 * q + a
                            last = tr(PJ[q % 2][:, a * T + s * P:a * T + (s + 1) * P],
                                      ntok[:, s, k * P:(k + 1) * P], ident[:, :])
                    last.then_inc(n_turned, 1)
                for q in range(2):
                    pe.wait_ge(nT_copied[q], 2 * base + 2)

            def compress(item):
                v = item[1]
                arrive(pe, item)
                if v == 0:
                    pe.wait_ge(proj_taken[0], 1)
                w = ring[:, loads[item][0], :].rearrange("p (i n) -> p i n", i=LT)
                for i in range(LT):
                    last = mm(PT[v][:, 0:NG], w[:, i, :], kpe[:, v, i, :], start=(i == 0), stop=(i == LT - 1))
                last.then_inc(hid_done, 1)

            def gates():
                pe.wait_ge(mod_done, 1)
                for s in range(TT):
                    for k in range(KD):
                        mm(OB[0][:, 24 * s:24 * s + 24], nT[:, k, s * P:(s + 1) * P], wgate[:, k, 0:24],
                           start=(k == 0), stop=(k == KD - 1), skip_group_check=True)
                for a in range(2):
                    for k in range(KD):
                        last = mm((OB[0], SC[0])[a][0:MH, 64:64 + T], wgate[:, k, 24 + MH * a:24 + MH * (a + 1)],
                                  nT[:, k, :], start=(k == 0), stop=(k == KD - 1), skip_group_check=True)
                last.then_inc(gates_done, 1)

            def gate_cols():
                pe.wait_ge(grow_done, 1)
                for a in range(2):
                    for s in range(TT):
                        last = tr(SC[1][:, 8 * a + 4 * s:8 * a + 4 * s + 4],
                                  grow[:, 5 + a, s * P:(s + 1) * P], ident[0:MH, 0:MH])
                last.then_inc(gcol_turned, 1)

            def cmp_keys():
                pe.wait_ge(hid_act, 1)
                mm(PT[0][:, 64:64 + NG], cw2d, hid[:, 0, :], start=True, stop=True)
                for g in range(2):
                    last = mm(PT[0][0:NCMP, 128 + DH * g:128 + DH * (g + 1)], hid[:, 1, g * NCMP:(g + 1) * NCMP],
                              cw2[:, 1, :], start=True, stop=True)
                last.then_inc(cmp_kv, 1)

            def cmp_scores():
                pe.wait_ge(cmp_kv_sb, 1)
                pe.wait_ge(gexp_done, 1)
                pe.wait_ge(grow_done, 1)
                for s in range(TT):
                    for r, g in ((r, g) for r in range(NR) for g in range(2)):
                        o = (s * NR + r) * NCMP
                        last = mm((OB[0], SC[0])[g][:, o:o + NCMP], qT[64 * g:64 * g + 64, r, s * P:(s + 1) * P],
                                  kcT[64 * g:64 * g + 64, g * NCMP:(g + 1) * NCMP], start=True, stop=True,
                                  skip_group_check=True)
                last.then_inc(cmp_score, 1)

            def head_scores(h):
                g, r = divmod(h, NR)
                if h == 0:
                    pe.wait_ge(masks, MASKS)
                    pe.wait_ge(gcol_done, 1)
                    pe.wait_ge(cmp_sub, 1)
                else:
                    pe.wait_ge(exp_done, h)
                for s in range(TT):
                    n = (s + 1) * P
                    for b in range(2):
                        mm(SC[s][:, b * T:b * T + n], qT[64 * g:64 * g + 64, r, s * P:(s + 1) * P],
                           kT[64 * g:64 * g + 64, b, 0:n], start=True, stop=False, skip_group_check=True)
                        last = mm(SC[s][:, b * T + s * P:b * T + n], identb[:, :], cmaskb[:, :],
                                  start=False, stop=True, skip_group_check=True)
                last.then_inc(score_done, 1)

            def head_turn(h):
                pe.wait_ge(probs_done, h + 1)
                if h == 0:
                    pe.wait_ge(cmp_p, 1)
                for b in range(2):
                    for n, (s_, t_) in enumerate(((0, 0), (0, 1), (1, 1))):
                        tr(PT[b][:, n * P:(n + 1) * P], Pb[:, h % 2, t_, b, s_ * P:(s_ + 1) * P], ident[:, :])
                    last = tr(PT[b][0:NCMP, 384:512], Pc[:, b, h, :], ident[:, :])
                last.then_inc(pt_done, 1)

            def head_out(h):
                g = h // NR
                j, half = divmod(h, 2)
                o = OB[0][64 * half:64 * half + 64, :]
                at = (0, 64 * half)
                pe.wait_ge(pt_copied[0], h + 1)
                pe.wait_ge(pt_copied[1], h + 1)
                if half == 0 and j:
                    pe.wait_ge(o_copied, j)
                for b in range(2):
                    mm(o[:, 0:T], vS[:, 0, b, 64 * g:64 * g + 64], PTb[:, b, 0:T],
                       start=(b == 0), stop=False, tile_position=at, skip_group_check=True)
                    mm(o[:, P:T], vS[:, 1, b, 64 * g:64 * g + 64], PTb[:, b, T:T + P],
                       start=False, stop=False, tile_position=at, skip_group_check=True)
                mm(o[:, 0:T], vc[0:NCMP, g, :], PcT[0:NCMP, :],
                   start=False, stop=True, tile_position=at, skip_group_check=True).then_inc(o_done, 1)

            def ml_scores(m):
                if m == 0:
                    pe.wait_ge(conv_act, 4)
                    pe.wait_ge(exp_done, NH)
                for s in range(TT):
                    n = T - s * P
                    mm(SC[s][:, 0:n], sel4[:, m, :], grow[:, 4, s * P:T], start=True, stop=False, skip_group_check=True)
                    mm(SC[s][:, 0:P], identb[:, :], tmaskb[:, :], start=False, stop=True, skip_group_check=True)
                    last = mm(SC[s][:, T:T + n], mlc[:, MH + m, s * P:(s + 1) * P], mlc[:, m, s * P:T],
                              start=True, stop=True, skip_group_check=True)
                last.then_inc(mls_done, 1)

            def ml_out(m):
                pe.wait_ge(mpt_done, m + 1)
                if m:
                    pe.wait_ge(hml_done, m)
                mm(PT[0][:, 0:129], MPT[:, 0:P], mlv[:, 0, m, :], start=True, stop=True, skip_group_check=True)
                mm(PT[0][:, 129:258], MPT[:, P:2 * P], mlv[:, 0, m, :], start=True, stop=False, skip_group_check=True)
                mm(PT[0][:, 129:258], MPT[:, 2 * P:3 * P], mlv[:, 1, m, :],
                   start=False, stop=True, skip_group_check=True).then_inc(num_done, 1)

            def ml_turn():
                pe.wait_ge(hml_norm, 1)
                for m in range(MH):
                    for s in range(TT):
                        last = tr(SC[m // 2][:, (m % 2) * T + s * P:(m % 2) * T + (s + 1) * P],
                                  hml[:, s, m * P:(m + 1) * P], ident[:, :])
                last.then_inc(mlT_turned, 1)

            def up(item):
                a = item[1]
                arrive(pe, item)
                if a == 0:
                    pe.wait_ge(o_copied, 4)
                    for b in range(2):
                        pe.wait_ge(proj_taken[b], (n_proj + 1 - b) // 2)
                else:
                    pe.wait_ge(mlT_copied, MH)
                s0 = loads[item][0]
                w = ring[:, s0:s0 + 2, :].rearrange("p a (k n) -> p (a k) n", n=D)
                src = (oT, mlT)[a]
                for q in range(4):
                    if a or q >= 2:
                        pe.wait_ge(up_taken, 4 * a + q - 1)
                    for i in range(2):
                        for k in range(4):
                            last = mm(PJ[q % 2][:, i * T:(i + 1) * T], w[:, k, (2 * q + i) * P:(2 * q + i + 1) * P],
                                      src[:, k, :], start=(k == 0), stop=(k == 3), skip_group_check=True)
                    last.then_inc(up_done, 1)

            def rows2(r):
                if r == 0:
                    pe.wait_ge(mod_done, 3)
                    pe.wait_ge(merged_done, 1)
                else:
                    pe.wait_ge(rows_used, 2)
                    pe.wait_ge(rows_used_act, 1)
                for j, bank in enumerate((PT[0], PT[1], SC[0], SC[1])):
                    last = spread(bank, 1 + r, j)
                last.then_inc(rows_done, 1)

            def mix(item):
                i = item[1]
                arrive(pe, item)
                w = ring[:, loads[item][0], :].rearrange("p (k n) -> p k n", n=D)
                for kk in range(2):
                    k = 2 * i + kk
                    for s in range(TT):
                        for half in range(2):
                            last = mm((OB, PJ)[s][half][:, :], merged[:, k, s * P:(s + 1) * P],
                                      w[:, kk, half * HD:(half + 1) * HD],
                                      start=(k == 0), stop=(k == KD - 1), skip_group_check=True)
                last.then_inc(mix_chunk, 1)

            def router():
                for s in range(TT):
                    for k in range(KD):
                        last = mm(SC[0][:, NE * s:NE * (s + 1)], nT[:, k, s * P:(s + 1) * P], wr[:, k, :],
                                  start=(k == 0), stop=(k == KD - 1), skip_group_check=True)
                last.then_inc(router_done, 1)
                pe.wait_ge(memb_done, 1)
                mm(SC[1][:, 0:NE], lower[:, :], memb[:, 0, :], start=True, stop=True, skip_group_check=True)
                mm(SC[1][:, NE:2 * NE], ones[:, :], memb[:, 0, :], start=True, stop=False, skip_group_check=True)
                mm(SC[1][:, NE:2 * NE], lower[:, :], memb[:, 1, :], start=False, stop=True, skip_group_check=True)
                mm(SC[1][0:1, 64:64 + NE], ones[:, 0:1], memb[:, 0, :], start=True, stop=False, skip_group_check=True)
                mm(SC[1][0:1, 64:64 + NE], ones[:, 0:1], memb[:, 1, :],
                   start=False, stop=True, skip_group_check=True).then_inc(rank_psum, 1)
                for s in range(TT):
                    last = tr(XB[0:NE, s * P:(s + 1) * P], gate[:, s, :], ident[:, :])
                last.then_inc(gatesT_psum, 1)
                pe.wait_ge(gatesT_done, 1)
                pe.wait_ge(moe_in, 16 * 4)
                for s in range(TT):
                    for half in range(2):
                        mm(ACC[s][half][:, :], gatesT[:, s * P:(s + 1) * P], b2all[:, half * HD:(half + 1) * HD],
                           start=True, stop=False, skip_group_check=True)

            for item in sched:
                kind = item[0]
                if kind == "small":
                    small_rows()
                elif kind == "params":
                    params()
                elif kind == "ada":
                    ada(item)
                elif kind == "rows1":
                    pe.wait_ge(mod_done, 1)
                    for j, bank in enumerate((SC[0], SC[1], PT[0], PT[1])):
                        last = spread(bank, 0, j)
                    last.then_inc(rows_done, 1)
                elif kind == "turn":
                    turn_n(item[1])
                elif kind == "proj":
                    project(item)
                elif kind == "gates":
                    gates()
                elif kind == "compress":
                    compress(item)
                elif kind == "gate_cols":
                    gate_cols()
                elif kind == "cmp_keys":
                    cmp_keys()
                elif kind == "cmp_scores":
                    cmp_scores()
                elif kind == "head_scores":
                    head_scores(item[1])
                elif kind == "head_turn":
                    head_turn(item[1])
                elif kind == "head_out":
                    head_out(item[1])
                elif kind == "ml_scores":
                    ml_scores(item[1])
                elif kind == "ml_out":
                    ml_out(item[1])
                elif kind == "ml_turn":
                    ml_turn()
                elif kind == "up":
                    up(item)
                elif kind == "rows2":
                    rows2(item[1])
                elif kind == "mix":
                    mix(item)
                elif kind == "router":
                    router()

            def gather(num):
                pe.wait_ge(hot_done, num)
                for s in range(TT):
                    for half in range(2):
                        last = mm(XB[64 * half:64 * half + 64, :], onehot[:, s, :],
                                  ntok[:, s, half * HD:(half + 1) * HD],
                                  start=(s == 0), stop=(s == TT - 1), tile_position=(0, 64 * half),
                                  skip_group_check=True)
                last.then_inc(gathered, 1)

            def turn_gathered():
                for m in range(4):
                    last = tr(YB[:, m * P:(m + 1) * P], xg[:, m * P:(m + 1) * P], ident[:, :])
                last.then_inc(xg_turned, 1)

            def bias():
                for q, bank in enumerate((HG, HL)):
                    for half in range(2):
                        last = mm(bank[64 * half:64 * half + 64, :], sel_e[:, :],
                                  b1all[:, q * D + half * HD:q * D + (half + 1) * HD],
                                  start=True, stop=False, tile_position=(0, 64 * half), skip_group_check=True)
                last.then_inc(biased, 1)

            def add_block():
                for s in range(TT):
                    for half in range(2):
                        last = mm(ACC[s][half][:, :], GT[64 * half:64 * half + 64, s * P:(s + 1) * P],
                                  ysb[64 * half:64 * half + 64, :], start=False, stop=False,
                                  tile_position=(64 * half, 0), skip_group_check=True)
                return last

            gather(1)
            pe.wait_ge(xg_copied, 1)
            turn_gathered()
            bias()

            def expert_block(e, num, b, main):
                pe.wait_ge(xgT_copied, num)
                for k in range(KD):
                    s = (MOE0 + k) % RING
                    pe.wait_ge(arrived[s], e * 16 + (per_slot[s] + 16))
                    for q, bank in enumerate((HG, HL)):
                        for half in range(2):
                            last = mm(bank[64 * half:64 * half + 64, :], xgT[:, k % 4, k // 4, :],
                                      ring[:, s, q * D + half * HD:q * D + (half + 1) * HD],
                                      start=False, stop=(k == KD - 1), tile_position=(0, 64 * half),
                                      skip_group_check=True)
                    if k == KD - 1:
                        last.then_inc(h_psum, 1)
                    elif main:
                        last.then_inc(ring_free, 1)
                gather(num + 1)
                pe.wait_ge(y_copied, num)
                pe.wait_ge(gt_copied, num)
                add_block()
                pe.wait_ge(onegate_done, num)
                for s in range(TT):
                    last = tr(YB[:, s * P:(s + 1) * P], onegate[:, s, :], ident[:, :])
                last.then_inc(gt_turned, 1)
                pe.wait_ge(act_made, num)
                pe.wait_ge(xg_copied, num + 1)
                for m in range(4):
                    last = tr(XB[:, m * P:(m + 1) * P], act_t[:, m * P:(m + 1) * P], ident[:, :])
                last.then_inc(act_turned, 1)
                pe.wait_ge(gt_copied, num + 1)
                turn_gathered()
                bias()
                pe.wait_ge(actT_copied, num)
                pe.wait_ge(xgT_copied, num + 1)
                for k in range(KD):
                    s = (MOE0 + KD + k // 2) % RING
                    if k % 2 == 0:
                        pe.wait_ge(arrived[s], e * 16 + (per_slot[s] + 16))
                    for half in range(2):
                        last = mm(YB[64 * half:64 * half + 64, :], actT[:, k % 4, k // 4, :],
                                  ring[:, s, (k % 2) * D + half * HD:(k % 2) * D + (half + 1) * HD],
                                  start=(k == 0), stop=(k == KD - 1), tile_position=(0, 64 * half),
                                  skip_group_check=True)
                    if k % 2 == 1 and k < KD - 1 and main:
                        last.then_inc(ring_free, 1)
                last.then_inc(y_psum, 1)

            pe.wait_ge(table_done, 1)
            each_block(pe, expert_block)
            total = pe.value_load(blk_t[0:1, NE:NE + 1], min_val=1, max_val=NBLK * NE)
            pe.wait_ge(y_copied, total + 1)
            pe.wait_ge(gt_copied, total + 1)
            add_block().then_inc(added, 1)

        @block.scalar
        def _(act):
            A = act.activation
            state = {"proj": 0}

            act.dma_start(rowA[:, 0, :], norm1_g.rearrange("(a d) -> a d", a=1).to_broadcast([P, D])).then_inc(gains_in, 16)
            for j in range(4):
                act.dma_start(modrow[32 * j:32 * j + 32, :, :],
                              ada_b.rearrange("(a p j n) -> a p j n", a=1, p=3, j=4)[:, :, j, :].to_broadcast([32, 3, 512])
                              ).then_inc(adab_in, 16)

            def squares(i):
                if i == 0:
                    act.wait_ge(x_in, 16)
                elif i == 1:
                    act.wait_ge(h_done, 1)
                for s in range(TT):
                    last = A(sqj[:, s, :], xres[:, s, :], ACT.Square, accum_out=ssq[:, s:s + 1])
                last.then_inc(ssq_done[i], 1)
                act.wait_ge(var_done[i], 1)
                A(std, ssq, ACT.Sqrt).then_inc(std_done[i], 1)

            def taken(n=1):
                b = state["proj"] % 2
                state["proj"] += 1
                return proj_taken[b]

            for item in sched:
                kind = item[0]
                if kind == "small":
                    act.wait_ge(small_copied, 1)
                    A(csig, ccol, ACT.Tanh, scale=0.5).then_inc(c_exp, 1)
                elif kind == "norm":
                    squares(item[1])
                elif kind == "turn":
                    for q in (0, 2):
                        act.wait_ge(n_turned, 4 * item[1] + q + 1)
                        A(nT[:, 2 * q:2 * q + 2, :], PJ[0].rearrange("p (a t) -> p a t", a=2), ACT.Copy
                          ).then_inc(nT_copied[0], 1)
                elif kind == "proj":
                    col, n = item[1], state["proj"]
                    bank = PJ[n % 2]
                    pair = bank.rearrange("p (r t) -> p r t", r=2)
                    if col == C_KV:
                        state["proj"] += 1
                        continue
                    act.wait_ge(proj_done, n + 1)
                    if col < C_KV:
                        a = col // 256
                        A(qT[:, 2 * a:2 * a + 2, :], pair, ACT.Copy).then_inc(taken(), 1)
                    elif col < C_NG:
                        b = (col - C_KV) // 256 - 1
                        A(kT[:, b, :], bank[:, 0:T], ACT.Copy)
                        A(vS[:, :, b, :], bank[:, T:2 * T].rearrange("p (s e) -> p s e", s=TT), ACT.Copy
                          ).then_inc(taken(), 1)
                    elif col < C_V:
                        i = (col - C_QK) // 256
                        A(mlx[:, 2 * i:2 * i + 2, 3:], pair, ACT.Copy).then_inc(taken(), 1)
                    elif col < C_IF:
                        i = (col - C_V) // 256
                        for s in range(TT):
                            ins = A(mlv[:, s, 2 * i:2 * i + 2, 0:P],
                                    pair[:, s, :].rearrange("p (h e) -> p h e", h=2), ACT.Copy)
                        ins.then_inc(taken(), 1)
                    elif col < C_MG:
                        i = (col - C_O) // 256
                        A(mlo[:, :, i * 256:(i + 1) * 256], pair, ACT.Tanh, scale=0.5).then_inc(taken(), 1)
                    else:
                        i = (col - C_MG) // 256
                        A(sg[:, 2 * i:2 * i + 2, :], pair, ACT.Tanh, scale=0.5).then_inc(taken(), 1)
                elif kind == "gates":
                    act.wait_ge(gates_done, 1)
                    A(gn, OB[0][:, 0:48].rearrange("p (s n) -> p s n", s=TT), ACT.Tanh, scale=0.5).then_inc(gexp_done, 1)
                    act.wait_ge(ls_in, 1)
                    A(grow[:, 1, :], grow[:, 1, :], ACT.Exp, scale=-1.0).then_inc(ls_exp, 1)
                    act.wait_ge(ls_in, 2)
                    A(grow[:, 2, :], grow[:, 1, :], ACT.Ln).then_inc(ls_ln, 1)
                    act.wait_ge(nm_in, 1)
                    A(grow[:, 6, :], grow[:, 6, :], ACT.Exp, scale=-1.0).then_inc(grow_done, 1)
                elif kind == "conv_act":
                    i = item[1]
                    act.wait_ge(conv_done, i + 1)
                    A(mlx[:, 2 * i:2 * i + 2, 3:], mlc[:, 2 * i:2 * i + 2, :], ACT.Tanh, scale=0.5).then_inc(conv_exp, 1)
                elif kind == "cmp_keys":
                    pass
                elif kind == "compress" and item[1] == 1:
                    act.wait_ge(gelu_in, 1)
                    A(htmp, htmp, ACT.Tanh, scale=GELU_A / 2).then_inc(gelu_exp, 1)
                elif kind == "cmp_scores":
                    act.wait_ge(cmp_sub, 1)
                    A(Zc, Zc, ACT.Exp, scale=NSA_SCALE).then_inc(cmp_exp, 1)
                elif kind == "head_scores":
                    h = item[1]
                    act.wait_ge(max_done, h + 1)
                    if h >= 2:
                        act.wait_ge(pt_done, h - 1)
                    for s in range(TT):
                        n = (s + 1) * P
                        for b in range(2):
                            last = A(Pb[:, h % 2, s, b, 0:n], SC[s][:, b * T:b * T + n], ACT.Exp,
                                     bias=nmx[:, h, s, b:b + 1], scale=NSA_SCALE, accum_out=psum_p[:, h, s, b:b + 1])
                    last.then_inc(exp_done, 1)
                elif kind == "head_turn":
                    h = item[1]
                    act.wait_ge(pt_done, h + 1)
                    A(PTb[:, 0, :], PT[0][:, 0:384], ACT.Copy)
                    A(PcT[0:NCMP, 0:P], PT[0][0:NCMP, 384:512], ACT.Copy).then_inc(pt_copied[0], 1)
                elif kind == "head_out":
                    h = item[1]
                    if h % 2:
                        act.wait_ge(o_done, h + 1)
                        A(oT[:, h // 2, :], OB[0][:, 0:T], ACT.Copy).then_inc(o_copied, 1)
                elif kind == "ml_scores":
                    m = item[1]
                    act.wait_ge(mls_done, m + 1)
                    if m == 0:
                        act.wait_ge(gcol_done, 1)
                    else:
                        act.wait_ge(num_done, m)
                    A(MPT[:, 0:T], SC[0][:, 0:T], ACT.Exp, scale=-1.0, bias=gcol[:, 0, 0, m:m + 1])
                    A(MPT[:, T:T + P], SC[1][:, 0:P], ACT.Exp, scale=-1.0, bias=gcol[:, 0, 1, m:m + 1]
                      ).then_inc(mle_done, 1)
                elif kind == "ml_norm":
                    act.wait_ge(var_done[3], 1)
                    A(hstd, hss, ACT.Sqrt).then_inc(std_done[3], 1)
                elif kind == "ml_turn":
                    act.wait_ge(mlT_turned, 1)
                    for m in range(MH):
                        A(mlT[:, m, :], SC[m // 2][:, (m % 2) * T:(m % 2 + 1) * T], ACT.Copy, scale=ngc[:, m:m + 1]
                          ).then_inc(mlT_copied, 1)
                elif kind == "rows2":
                    act.wait_ge(rows_done, 2 + item[1])
                    if item[1] == 0:
                        A(rsh2[:, 0:512], SC[0][:, :], ACT.Copy)
                        A(rsh2[:, 512:1024], SC[1][:, :], ACT.Copy).then_inc(rows_used_act, 1)
                elif kind == "router":
                    act.wait_ge(top_done, 1)
                    for s in range(TT):
                        last = A(gexp[:, s, :], top8[:, s, 0:TOPK], ACT.Exp, bias=nmax[:, s:s + 1],
                                 accum_out=gsum[:, s:s + 1])
                    last.then_inc(top_exp, 1)
                    act.wait_ge(gatesT_psum, 1)
                    A(gatesT, XB[0:NE, 0:T], ACT.Copy).then_inc(gatesT_done, 1)

            act.wait_ge(table_done, 1)

            def take_gathered(num):
                act.wait_ge(gathered, num)
                A(xg, XB[:, :], ACT.Copy).then_inc(xg_copied, 1)

            def take_turned(num):
                act.wait_ge(xg_turned, num)
                A(xgT.rearrange("p m h s -> p (m h s)"), YB[:, :], ACT.Copy).then_inc(xgT_copied, 1)

            take_gathered(1)
            take_turned(1)

            def expert_block(e, num, b, main):
                act.wait_ge(glu_min, num)
                A(sgm, glu, ACT.Sigmoid, scale=ALPHA).then_inc(sig_glu, 1)
                take_gathered(num + 1)
                act.wait_ge(gt_turned, num)
                A(GT, YB[:, 0:T], ACT.Copy).then_inc(gt_copied, 1)
                take_turned(num + 1)
                act.wait_ge(y_psum, num)
                A(ysb, YB[:, :], ACT.Copy).then_inc(y_copied, 1)

            each_block(act, expert_block)
            act.wait_ge(h_done, 2)
            for s in range(TT):
                last = A(sqj[:, s, :], xres[:, s, :], ACT.Square, accum_out=ssq[:, s:s + 1])
            last.then_inc(ssq_done[2], 1)
            act.wait_ge(var_done[2], 1)
            A(std, ssq, ACT.Sqrt).then_inc(std_done[2], 1)

        @block.vector
        def _(dve):
            chain = [0]

            def link(ins):
                chain[0] += 1
                ins.then_inc(dve_chain, 1)
                dve.wait_ge(dve_chain, chain[0])

            tt_, ts_, stt_, cp = dve.tensor_tensor, dve.tensor_scalar, dve.scalar_tensor_tensor, dve.tensor_copy
            state = {"proj": 0}

            def root(i, ssq_, std_, rstd_, n):
                ts_(ssq_, ssq_, 1.0 / n, EPS, ALU.mult, ALU.add).then_inc(var_done[i], 1)
                dve.wait_ge(std_done[i], 1)
                link(dve.reciprocal(rstd_, std_))

            for item in sched:
                kind = item[0]
                if kind == "small":
                    dve.wait_ge(turned_c, 1)
                    cp(ccol, SC[0][:, 0:KD]).then_inc(small_copied, 1)
                    dve.wait_ge(c_exp, 1)
                    link(ts_(csig, csig, 1.0, 0.5, ALU.add, ALU.mult))
                    link(tt_(ccol, ccol, csig, ALU.mult))
                    cp(crep[:], ccol.rearrange("p (k o) -> p k o", o=1).to_broadcast([P, KD, 32])).then_inc(crep_done, 1)
                elif kind == "params":
                    dve.wait_ge(turned_small, 1)
                    link(cp(peT.rearrange("p v i -> p (v i)"), OB[1][:, 16:16 + 2 * LT]))
                    cp(convw.rearrange("p w m -> p (w m)"), OB[1][:, 64:96])
                    cp(convb, OB[1][:, 96:104])
                    ts_(ngc, OB[1][:, 104:108], 0.5, None, ALU.mult).then_inc(params_done, 1)
                    cp(cw2d.rearrange("p (a e) -> p a e", a=2),
                       cw2[:, 0, :].rearrange("p (a e) -> p a e", a=1).to_broadcast([P, 2, DH]))
                    link(dve.memset(grow[:, 7, :], 0.0))
                elif kind == "norm":
                    i = item[1]
                    dve.wait_ge(ssq_done[i], 1)
                    root(i, ssq, std, rstd, D)
                    for s in range(TT):
                        ins = ts_(ntok[:, s, :], xres[:, s, :], rstd[:, s:s + 1], None, ALU.mult)
                    link(ins)
                    if i == 1:
                        for half in range(2):
                            n_ = ntok[:, :, half * HD:(half + 1) * HD]
                            row = lambda a: a[:, half * HD:(half + 1) * HD].rearrange(
                                "p (a d) -> p a d", a=1).to_broadcast([P, TT, HD])
                            link(tt_(n_, n_, row(rs2), ALU.mult))
                            tt_(n_, n_, row(rsh2), ALU.add).then_inc(ntok_done, 1)
                elif kind == "mod":
                    p = item[1]
                    dve.wait_ge(ada_chunk, KD * (p + 1))
                    if p == 0:
                        dve.wait_ge(adab_in, 16 * 4)
                    tt_(modrow[:, p, :], modrow[:, p, :], OB[min(p, 1)][:, :], ALU.add).then_inc(mod_done, 1)
                elif kind == "rows1":
                    dve.wait_ge(rows_done, 1)
                    dve.wait_ge(gains_in, 16)
                    for half in range(2):
                        r = rowA[:, 0:1, half * HD:(half + 1) * HD]
                        n_ = ntok[:, :, half * HD:(half + 1) * HD]
                        flat = r.rearrange("p a d -> p (a d)")
                        link(stt_(flat, PT[half][:, :], 1.0, flat, ALU.add, ALU.mult))
                        link(tt_(n_, n_, r.to_broadcast([P, TT, HD]), ALU.mult))
                        tt_(n_, n_, SC[half].rearrange("p (a d) -> p a d", a=1).to_broadcast([P, TT, HD]), ALU.add
                            ).then_inc(ntok_done, 1)
                elif kind == "turn":
                    for q in (1, 3):
                        dve.wait_ge(n_turned, 4 * item[1] + q + 1)
                        cp(nT[:, 2 * q:2 * q + 2, :], PJ[1].rearrange("p (a t) -> p a t", a=2)).then_inc(nT_copied[1], 1)
                elif kind == "proj":
                    n = state["proj"]
                    state["proj"] += 1
                    if item[1] == C_KV:
                        dve.wait_ge(proj_done, n + 1)
                        for v in range(2):
                            for g in range(2):
                                for a in range(2):
                                    src = PJ[n % 2][64 * g:64 * g + 64, v * T:(v + 1) * T]
                                    out_ = kpe[64 * a:64 * a + 64, v, :, g * NCMP:(g + 1) * NCMP]
                                    pos_ = peT[64 * a:64 * a + 64, v, :]
                                    for hb in range(2):
                                        i0 = hb * LT // 2
                                        src_ = src[:, hb * STRIDE:hb * STRIDE + NCMP * STRIDE].rearrange(
                                            "p (n i a) -> p a i n", i=LT // 2, a=2)[:, a]
                                        ins = tt_(out_[:, i0:i0 + LT // 2, :], src_,
                                                  pos_[:, i0:i0 + LT // 2].rearrange("p (i o) -> p i o", o=1)
                                                  .to_broadcast([64, LT // 2, NCMP]), ALU.add)
                        ins.then_inc(proj_taken[n % 2], 1)
                elif kind == "gates":
                    dve.wait_ge(gates_done, 1)
                    link(ts_(grow[:, 0, :], SC[0][0:MH, 64:64 + T], gb[0:MH, 1:2], None, ALU.add))
                    stt_(grow[:, 1, :], grow[:, 0, :], -1.0, grow[:, 0, :], ALU.mult, ALU.max).then_inc(ls_in, 1)
                    dve.wait_ge(ls_exp, 1)
                    ts_(grow[:, 1, :], grow[:, 1, :], 1.0, None, ALU.add).then_inc(ls_in, 1)
                    dve.wait_ge(ls_ln, 1)
                    link(stt_(grow[:, 0, :], grow[:, 0, :], 0.0, grow[:, 2, :], ALU.min, ALU.subtract))
                    link(dve.tensor_tensor_scan(grow[:, 3, :], grow[:, 0, :], grow[:, 7, :], 0.0, ALU.add, ALU.add))
                    dve.wait_ge(gexp_done, 1)
                    link(stt_(grow[:, 5, :], OB[0][0:MH, 64:64 + T], gb[0:MH, 0:1], grow[:, 3, :], ALU.add, ALU.subtract))
                    link(dve.tensor_tensor_scan(grow[:, 4, :], grow[:, 5, :], grow[:, 5, :], 0.0, ALU.max, ALU.max))
                    tt_(grow[:, 6, :], grow[:, 3, :], grow[:, 4, :], ALU.add).then_inc(nm_in, 1)
                    link(ts_(gn, gn, 1.0, 0.5, ALU.add, ALU.mult))
                elif kind == "gate_cols":
                    dve.wait_ge(gcol_turned, 1)
                    cp(gcol.rearrange("p a s h -> p (a s h)"), SC[1][:, 0:16]).then_inc(gcol_done, 1)
                elif kind == "conv":
                    i = item[1]
                    if i == 0:
                        dve.wait_ge(masks, MASKS)
                    n = state["proj"] - 1
                    dve.wait_ge(proj_taken[n % 2], n // 2 + 1)
                    for w in (3, 2, 1, 0):
                        for m in (2 * i, 2 * i + 1):
                            if w == 3:
                                ins = ts_(mlc[:, m, :], mlx[:, m, 3:3 + T], convw[:, 3, m:m + 1], convb[:, m:m + 1],
                                          ALU.mult, ALU.add)
                            else:
                                ins = stt_(mlc[:, m, :], mlx[:, m, w:w + T], convw[:, w, m:m + 1], mlc[:, m, :],
                                           ALU.mult, ALU.add)
                        if w:
                            link(ins)
                    ins.then_inc(conv_done, 1)
                elif kind == "conv_act":
                    i = item[1]
                    dve.wait_ge(conv_exp, i + 1)
                    ex, cc = mlx[:, 2 * i:2 * i + 2, 3:], mlc[:, 2 * i:2 * i + 2, :]
                    stt_(cc, ex, 1.0, cc, ALU.add, ALU.mult).then_inc(conv_act, 1)
                elif kind == "compress" and item[1] == 1:
                    dve.wait_ge(hid_done, 2)
                    for v in range(2):
                        ins = cp(hid[:, v, :], PT[v][:, 0:NG])
                    link(ins)
                    link(tt_(htmp, hid, hid, ALU.mult))
                    link(ts_(htmp, htmp, GELU_B, 1.0, ALU.mult, ALU.add))
                    tt_(htmp, htmp, hid, ALU.mult).then_inc(gelu_in, 1)
                    dve.wait_ge(gelu_exp, 1)
                    link(ts_(htmp, htmp, 1.0, 0.5, ALU.add, ALU.mult))
                    tt_(hid, hid, htmp, ALU.mult).then_inc(hid_act, 1)
                elif kind == "cmp_keys":
                    dve.wait_ge(cmp_kv, 1)
                    cp(kcT, PT[0][:, 64:64 + NG])
                    cp(vc[0:NCMP, :, :], PT[0][0:NCMP, 128:256].rearrange("p (g e) -> p g e", g=2)).then_inc(cmp_kv_sb, 1)
                elif kind == "cmp_scores":
                    dve.wait_ge(cmp_score, 1)
                    for g in range(2):
                        sc_ = (OB[0], SC[0])[g][:, 0:TT * NR * NCMP].rearrange("p (s h n) -> p s h n", s=TT, h=NR)
                        ins = tt_(Zc[:, :, g * NR:(g + 1) * NR, :], sc_, cneg[:, :, 0:NR, :], ALU.add)
                    link(ins)
                    link(dve.tensor_reduce(cmx, Zc, AX, ALU.max))
                    bc = lambda a: a.rearrange("p s (h o) -> p s h o", o=1).to_broadcast([P, TT, NH, NCMP])
                    tt_(Zc, Zc, bc(cmx), ALU.subtract).then_inc(cmp_sub, 1)
                    dve.wait_ge(cmp_exp, 1)
                    link(dve.tensor_reduce(csum, Zc, AX, ALU.add))
                    link(dve.reciprocal(csum, csum))
                    link(tt_(csum, csum, gn[:, :, 0:NH], ALU.mult))
                    link(tt_(Zc, Zc, c01, ALU.mult))
                    tt_(Pc, Zc, bc(csum), ALU.mult).then_inc(cmp_p, 1)
                elif kind == "head_scores":
                    h = item[1]
                    dve.wait_ge(score_done, h + 1)
                    for s in range(TT):
                        n = (s + 1) * P
                        ins = dve.tensor_reduce(mx[:, h, s, :], SC[s].rearrange("p (b t) -> p b t", b=2)[:, :, 0:n],
                                                AX, ALU.max)
                    link(ins)
                    ts_(nmx[:, h], mx[:, h], -NSA_SCALE, None, ALU.mult).then_inc(max_done, 1)
                    dve.wait_ge(exp_done, h + 1)
                    link(dve.reciprocal(rsc[:, h], psum_p[:, h]))
                    link(tt_(rsc[:, h], rsc[:, h], gn[:, :, NH + h:3 * NH:NH], ALU.mult))
                    for s in range(TT):
                        n = (s + 1) * P
                        pp = Pb[:, h % 2, s, :, 0:n]
                        ins = tt_(pp, pp, rsc[:, h, s, :].rearrange("p (b o) -> p b o", o=1).to_broadcast([P, 2, n]), ALU.mult)
                    ins.then_inc(probs_done, 1)
                elif kind == "head_turn":
                    h = item[1]
                    dve.wait_ge(pt_done, h + 1)
                    cp(PTb[:, 1, :], PT[1][:, 0:384])
                    cp(PcT[0:NCMP, P:2 * P], PT[1][0:NCMP, 384:512]).then_inc(pt_copied[1], 1)
                elif kind == "ml_scores":
                    m = item[1]
                    dve.wait_ge(mle_done, m + 1)
                    stt_(MPT[:, 0:T], SC[0][:, T:2 * T], ML_SCALE / 4, MPT[:, 0:T], ALU.mult, ALU.mult)
                    stt_(MPT[:, T:T + P], SC[1][:, T:T + P], ML_SCALE / 4, MPT[:, T:T + P], ALU.mult, ALU.mult
                         ).then_inc(mpt_done, 1)
                elif kind == "ml_out":
                    m = item[1]
                    dve.wait_ge(num_done, m + 1)
                    nd = PT[0][:, 0:258].rearrange("p (s e) -> p s e", s=TT)
                    d_ = den[:, m, :].rearrange("p (s o) -> p s o", o=1)
                    link(cp(d_, nd[:, :, 128:129]))
                    link(stt_(d_, d_, -1.0, d_, ALU.mult, ALU.max))
                    link(tt_(d_, d_, gcol[:, 1, :, m:m + 1], ALU.max))
                    link(dve.reciprocal(d_, d_))
                    tt_(hml[:, :, m * P:(m + 1) * P], nd[:, :, 0:P], d_.to_broadcast([P, TT, P]), ALU.mult
                        ).then_inc(hml_done, 1)
                elif kind == "ml_norm":
                    dve.wait_ge(hml_done, MH)
                    link(tt_(hsq, hml, hml, ALU.mult))
                    link(dve.tensor_reduce(hss, hsq.rearrange("p s (h e) -> p (s h) e", h=MH), AX, ALU.add))
                    root(3, hss, hstd, hr, P)
                    h4 = hml.rearrange("p s (h e) -> p (s h) e", h=MH)
                    link(tt_(h4, h4, hr.rearrange("p (n o) -> p n o", o=1).to_broadcast([P, TT * MH, P]), ALU.mult))
                    dve.wait_ge(proj_taken[0], (n_proj + 1) // 2)
                    dve.wait_ge(proj_taken[1], n_proj // 2)
                    stt_(hml, mlo, 1.0, hml, ALU.add, ALU.mult).then_inc(hml_norm, 1)
                elif kind == "up":
                    a = item[1]
                    for q in range(4):
                        dve.wait_ge(up_done, 4 * a + q + 1)
                        pair = PJ[q % 2].rearrange("p (i t) -> p i t", i=2)
                        dst = merged[:, 2 * q:2 * q + 2, :]
                        if a == 0:
                            stt_(dst, sg[:, 2 * q:2 * q + 2, :], 1.0, pair, ALU.add, ALU.mult).then_inc(up_taken, 1)
                        else:
                            tmp = mtmp.rearrange("p (i t) -> p i t", i=2)
                            ins = stt_(tmp, sg[:, 8 + 2 * q:8 + 2 * q + 2, :], 1.0, pair, ALU.add, ALU.mult)
                            ins.then_inc(up_taken, 1)
                            dve.wait_ge(up_taken, 4 + q + 1)
                            ins = tt_(dst, dst, tmp, ALU.add)
                            if q < 3:
                                link(ins)
                    if a:
                        ins.then_inc(merged_done, 1)
                elif kind == "rows2":
                    dve.wait_ge(rows_done, 2 + item[1])
                    banks = (PT[0], PT[1], SC[0], SC[1])
                    if item[1] == 0:
                        for half in range(2):
                            ts_(rg1[:, half * HD:(half + 1) * HD], PT[half][:, :], 1.0, 0.5, ALU.add, ALU.mult).then_inc(rows_used, 1)
                    else:
                        dve.wait_ge(moe_in, 16 * 4)
                        for half in range(2):
                            r = rg2[:, half * HD:(half + 1) * HD]
                            ins = stt_(rs2[:, half * HD:(half + 1) * HD], PT[half][:, :], 1.0, r, ALU.add, ALU.mult)
                        link(ins)
                        for half in range(2):
                            ins = ts_(rg2[:, half * HD:(half + 1) * HD], SC[half][:, :], 1.0, None, ALU.add)
                        link(ins)
                elif kind == "add_mix":
                    dve.wait_ge(mix_chunk, KD // 2)
                    for s in range(TT):
                        for half in range(2):
                            ins = tt_(ntok[:, s, half * HD:(half + 1) * HD], (OB, PJ)[s][half][:, :],
                                      rg1[:, half * HD:(half + 1) * HD], ALU.mult)
                    link(ins)
                    tt_(xres[:], xres[:], ntok[:], ALU.add).then_inc(h_done, 1)
                elif kind == "router":
                    dve.wait_ge(router_done, 1)
                    link(tt_(logit, SC[0][:, 0:2 * NE].rearrange("p (s e) -> p s e", s=TT),
                             rbias.rearrange("p (a e) -> p a e", a=1).to_broadcast([P, TT, NE]), ALU.add))
                    for s in range(TT):
                        ins = dve.max(top8[:, s, :], logit[:, s, :])
                    link(ins)
                    ts_(nmax, top8[:, :, 0], -1.0, None, ALU.mult).then_inc(top_done, 1)
                    for s in range(TT):
                        ins = dve.max_index(idx8[:, s, :], top8[:, s, :], logit[:, s, :])
                    link(ins)
                    link(cp(idxf[:], idx8[:]))
                    dve.wait_ge(top_exp, 1)
                    link(dve.reciprocal(grs, gsum))
                    for s in range(TT):
                        ins = ts_(gexp[:, s, :], gexp[:, s, :], grs[:, s:s + 1], None, ALU.mult)
                    link(ins)
                    ie = iota_f[:, 0, 0, 0:NE]
                    dve.wait_ge(iota_made, 1)
                    for s in range(TT):
                        for j in range(TOPK):
                            if j == 0:
                                ts_(memb[:, s, :], ie, idxf[:, s, 0:1], None, ALU.is_equal)
                                link(ts_(gate[:, s, :], ie, idxf[:, s, 0:1], gexp[:, s, 0:1], ALU.is_equal, ALU.mult))
                            else:
                                stt_(memb[:, s, :], ie, idxf[:, s, j:j + 1], memb[:, s, :], ALU.is_equal, ALU.add)
                                link(ts_(wtmp, ie, idxf[:, s, j:j + 1], gexp[:, s, j:j + 1], ALU.is_equal, ALU.mult))
                                ins = tt_(gate[:, s, :], gate[:, s, :], wtmp, ALU.add)
                                if (s, j) != (TT - 1, TOPK - 1):
                                    link(ins)
                    ins.then_inc(memb_done, 1)
                    dve.wait_ge(rank_psum, 1)
                    link(dve.memset(rank, -1.0))
                    rk = rank[:, :, 0:NE]
                    link(stt_(rk, SC[1][:, 0:2 * NE].rearrange("p (s e) -> p s e", s=TT), 1.0, memb, ALU.add, ALU.mult))
                    link(ts_(rk, rk, -1.0, None, ALU.add))
                    cnt, nblk, upto, zero = (cntf[0:1, a, :] for a in range(4))
                    link(cp(cnt, SC[1][0:1, 64:64 + NE]))
                    dve.memset(zero, 0.0)
                    link(ts_(nblk, cnt, SLOTS + 0.5, 1.0, ALU.is_gt, ALU.add))
                    for b in range(2, NBLK):
                        link(stt_(nblk, cnt, SLOTS * b + 0.5, nblk, ALU.is_gt, ALU.add))
                    link(dve.tensor_tensor_scan(upto, nblk, zero, 0.0, ALU.add, ALU.add))
                    cp(cnt_t[:], cnt)
                    dve.memset(blk_t[0:1, 0:1], 0)
                    link(dve.memset(next_t[:], 0))
                    for b in range(NBLK - 1):
                        ts_(next_t[0:1, b, 0:NE], cnt, SLOTS * (b + 1) + 0.5, float(b + 1), ALU.is_gt, ALU.mult)
                    cp(blk_t[0:1, 1:NE + 1], upto).then_inc(table_done, 1)

            dve.wait_ge(table_done, 1)

            def make_hot(e_, b_):
                hot = iota_f[:, bass.ds(b_, 1), 0, :].rearrange("p a n -> p (a n)")
                for s in range(TT):
                    ts_(onehot[:, s, :], hot, rank[:, s, bass.ds(e_, 1)], None, ALU.is_equal)
                cp(sel_e, ident[0:NE, bass.ds(e_, 1)].to_broadcast([NE, SLOTS])).then_inc(hot_done, 1)

            make_hot(0, dve.value_load(next_t[0:1, 0, 0:1], min_val=0, max_val=NBLK - 1))
            dve.memset(ysb, 0.0).then_inc(y_copied, 1)
            dve.wait_ge(gatesT_done, 1)
            dve.memset(GT, 0.0).then_inc(gt_copied, 1)

            def expert_block(e, num, b, main):
                after = e + 1 if main else e
                b_after = dve.value_load(next_t[0:1, b, bass.ds(after, 1)], min_val=0, max_val=NBLK - 1)
                dve.wait_ge(biased, num)
                make_hot(after, b_after)
                hot = iota_f[:, b, :, :].rearrange("p a n -> p (a n)")
                for s in range(TT):
                    ins = ts_(onegate[:, s, :], hot, rank[:, s, bass.ds(e, 1)], gate[:, s, bass.ds(e, 1)],
                              ALU.is_equal, ALU.mult)
                ins.then_inc(onegate_done, 1)
                dve.wait_ge(h_psum, num)
                ts_(glu, HG[:, :], LIMIT, None, ALU.min).then_inc(glu_min, 1)
                ts_(lin, HL[:, :], LIMIT, -LIMIT, ALU.min, ALU.max)
                dve.wait_ge(sig_glu, num)
                tt_(glu, glu, sgm, ALU.mult).then_inc(glu_gated, 1)
                dve.wait_ge(glu_gated, num)
                stt_(act_t, lin, 1.0, glu, ALU.add, ALU.mult).then_inc(act_made, 1)
                dve.wait_ge(act_turned, num)
                cp(actT.rearrange("p m h s -> p (m h s)"), XB[:, :]).then_inc(actT_copied, 1)

            each_block(dve, expert_block)
            dve.wait_ge(added, 1)
            for s in range(TT):
                for half in range(2):
                    ins = tt_(otmp[:, s, half * HD:(half + 1) * HD], ACC[s][half][:, :],
                              rg2[:, half * HD:(half + 1) * HD], ALU.mult)
            link(ins)
            tt_(xres[:], xres[:], otmp, ALU.add).then_inc(h_done, 1)
            dve.wait_ge(ssq_done[2], 1)
            root(2, ssq, std, rstd, D)
            dve.wait_ge(rfin_in, 16)
            for s in range(TT):
                stt_(otmp[:, s, :], xres[:, s, :], rstd[:, s:s + 1], rfin, ALU.mult, ALU.mult).then_inc(final_done, 1)


_INS = ['x', 'c', 'ada_w', 'ada_b', 'norm1_g', 'w_in', 'nsa_pe_k', 'nsa_pe_v', 'nsa_cmp_w1_k', 'nsa_cmp_w2_k',
        'nsa_cmp_w1_v', 'nsa_cmp_w2_v', 'ml_conv_w', 'ml_conv_b', 'ml_gate_b', 'ml_norm_g', 'w_up_nsa', 'w_up_ml',
        'w_out', 'norm2_g', 'router_w', 'router_b', 'exp_w1', 'exp_b1', 'exp_w2', 'exp_b2', 'final_g']


def kernel(**inputs):
    import numpy as _np
    import concourse.bacc as _bacc
    from concourse import mybir as _mybir
    from concourse.bass_utils import run_bass_kernel_spmd as _run

    nc = _bacc.Bacc("TRN2", target_bir_lowering=False, num_devices=1)
    arrays, args = {}, []
    for name in _INS:
        a = _np.ascontiguousarray(inputs[name])
        if name not in ('c', 'final_g'):
            a = a[0]
        arrays[f"in_{name}_dram"] = a
        args.append(nc.dram_tensor(f"in_{name}_dram", a.shape, _mybir.dt.from_np(a.dtype), kind="ExternalInput").ap())
    shape = inputs['x'].shape
    args.append(nc.dram_tensor("out_0_dram", shape[1:], _mybir.dt.float32, kind="ExternalOutput").ap())
    hybrid_block(nc, *args)
    r = _run(nc, [arrays], core_ids=[0])
    return r.results[0]["out_0_dram"].reshape(shape)
```

```python
from contextlib import ExitStack

import concourse.bass as bass
from concourse import mybir

ALU = mybir.AluOpType
ACT = mybir.ActivationFunctionType
F32 = mybir.dt.float32
BF16 = mybir.dt.bfloat16
I32 = mybir.dt.int32
U32 = mybir.dt.uint32
AX = mybir.AxisListType.X

P = 128


def hybrid_block(nc, x, c, ada_w, ada_b, norm1_g, w_in, pe_k, pe_v, cw1_k, cw2_k, cw1_v, cw2_v,
                 conv_w, conv_b, gate_b, norm_g, w_up_nsa, w_up_ml, w_out, norm2_g,
                 router_w, router_b, exp_w1, exp_b1, exp_w2, exp_b2, final_g, out):
    T, D = x.shape
    TT, KD = T // P, D // P
    HD = D // 2
    NH, DH = 8, 64
    NR = NH // 2
    MH = 4
    EPS = 1e-6
    NSA_SCALE = DH ** -0.5
    ML_SCALE = P ** -0.5
    STRIDE, CLEN = 16, 32
    NCMP = T // STRIDE - 1
    NG = 2 * NCMP
    LT = CLEN * DH // P
    NE = router_w.shape[1]
    TOPK = 4
    SLOTS = 64
    NBLK = T // SLOTS
    LIMIT, ALPHA = 7.0, 1.702
    GELU_A, GELU_B = 2.0 * (2.0 / 3.141592653589793) ** 0.5, 0.044715

    C_Q, C_KV, C_NG = 0, 512, 1280
    C_QK, C_V, C_IF, C_O, C_MG = 1304, 2328, 2840, 2848, 3360

    RING, EXTRA, RW = 12, 4, 2048
    MASKS, SMALL = 11, 16 * 5

    sched = [("small",), ("norm", 0)]
    sched += [("ada", 0, k) for k in range(4)] + [("turn", 0)] + [("ada", 0, k) for k in range(4, KD)]
    sched += [("mod", 0), ("mod_cols", 0), ("params",)]
    sched += [("proj", C_KV), ("proj", C_KV + 256), ("proj", C_KV + 512), ("proj", C_Q), ("proj", C_Q + 256), ("gate_sums",)]
    ada_left = [("ada", p, k) for p in (1, 2) for k in range(KD)]
    wide = [C_QK + 256 * i for i in range(4)] + [C_V, C_V + 256, C_O, C_O + 256]
    wide += [C_MG + 256 * i for i in range(8)]
    for i, col in enumerate(wide):
        sched.append(("proj", col))
        if i == 0:
            sched.append(("gates",))
        if i == 2:
            sched.append(("cmp_keys",))
        if i < 4:
            sched.append(("conv", i))
        if i == 0:
            sched += [("compress", 0), ("compress", 1)]
        if i == 1:
            sched += [("cmp_fold",), ("gate_cols",)]
        if i < 4:
            sched.append(("conv_act", i))
        if 0 <= i - 5 < NH:
            sched.append(("head_out", i - 5))
        if 0 <= i - 12 < MH:
            sched.append(("ml_out", i - 12))
        if 0 <= i - 4 < NH:
            sched.append(("head_turn", i - 4))
        if 0 <= i - 3 < NH:
            sched.append(("head_scores", i - 3))
        if 0 <= i - 11 < MH:
            sched.append(("ml_scores", i - 11))
        sched.append(ada_left.pop(0))
        if i == 2:
            sched.append(("cmp_scores",))
        if i == 7 or i == 15:
            sched.append(("mod", i // 8 + 1))
    sched += [("ml_norm",), ("up", 0), ("gate_rows", 0), ("ml_turn",), ("up", 1), ("mod_cols", 1), ("gate_evac",)]
    sched += [("mix", i) for i in range(KD // 2)] + [("mix_tile", 1, 0), ("second_norm", 0), ("mix_tile", 1, 1)]
    sched += [("logits", 0), ("gate_rows", 1), ("second_norm", 1), ("logits", 1), ("router",)]

    STREAMED = {"ada": 1, "proj": 1, "compress": 1, "up": 2, "mix": 1}

    def streamed_from(at_):
        for item in sched:
            n = STREAMED.get(item[0], 0)
            at_ += n + (at_ % RING + n > RING if n else 0)
        return at_

    first = next(a for a in range(RING) if streamed_from(a) % RING == 0)
    loads, order, at_, per_slot = {}, [], first, [0] * RING
    for item in sched:
        n = STREAMED.get(item[0], 0)
        if n:
            at_ += at_ % RING + n > RING
            s = at_ % RING
            per_slot[s] += 64 if item[0] == "proj" and item[1] < C_KV else 16
            loads[item] = (s, n, at_, per_slot[s])
            order.append(item)
            at_ += n
    MOE0 = at_
    PER_E = KD + KD // 2
    SPAN = RING + EXTRA
    TURN = next(n for n in range(1, NE) if PER_E * n % SPAN == 0)
    assert PER_E == RING and MOE0 % RING == 0 and NE % TURN == 0

    with ExitStack() as ctx:
        def sb(name, shape, dt=F32):
            return ctx.enter_context(nc.sbuf_tensor(name, shape, dt))

        def psum(name):
            return ctx.enter_context(nc.psum_tensor(name, [P, 512], F32))

        def sem(name):
            return ctx.enter_context(nc.semaphore(name))

        xres = sb("xres", [P, TT, D])
        ntok = sb("ntok", [P, TT, D])
        nT = sb("nT", [P, KD, T])
        ident = sb("ident", [P, P])
        identb = sb("identb", [P, P], BF16)
        cmaskb = sb("cmaskb", [P, P], BF16)
        tmaskb = sb("tmaskb", [P, P], BF16)
        sel0 = sb("sel0", [P, P])
        sel4 = sb("sel4", [MH, MH, P])
        fold = sb("fold", [P, 32])
        ones = sb("ones", [P, P])
        lower = sb("lower", [P, P])
        modrow = sb("modrow", [P, 3, 512])
        small = sb("small", [P, 276])
        crep = sb("crep", [P, KD, 32])
        wgate = sb("wgate", [P, KD, 32])

        ARENA = 18412
        stage = sb("stage", [P, RING * RW + ARENA])
        ring = stage[:, 0:(RING + EXTRA) * RW].rearrange("p (s n) -> p s n", n=RW)
        arena = stage[:, RING * RW:]
        used = {"f": 0, "m": 0}

        def view(side, n, parts=P):
            o = used[side]
            used[side] += n
            assert used[side] <= ARENA, (side, used[side])
            return arena[0:parts, o:o + n]

        sg = view("f", 16 * T).rearrange("p (m t) -> p m t", m=16)
        mlc = view("f", 8 * T).rearrange("p (m t) -> p m t", m=8)
        mlx = sg.rearrange("p m t -> p (m t)")[:, 0:8 * (T + 3)].rearrange("p (m t) -> p m t", m=8)
        qT = view("f", NR * T).rearrange("p (r t) -> p r t", r=NR)
        kT = view("f", 2 * T).rearrange("p (b t) -> p b t", b=2)
        vS = view("f", TT * 2 * P).rearrange("p (s b e) -> p s b e", s=TT, b=2)
        mlv = view("f", TT * MH * 129).rearrange("p (s h e) -> p s h e", s=TT, h=MH)
        mlo = view("f", TT * 512).rearrange("p (s e) -> p s e", s=TT)
        Pb = view("f", 2 * TT * 2 * T).rearrange("p (z s b t) -> p z s b t", z=2, s=TT, b=2)
        kpe = Pb.rearrange("p z s b t -> p (z s b t)")[:, 0:2 * LT * 32].rearrange(
            "p (v i n) -> p v i n", v=2, i=LT)
        PTb = view("f", 2 * 384).rearrange("p (b t) -> p b t", b=2)
        MPT = view("f", 384)
        PcT = view("f", 256)
        Pc = view("f", TT * NH * NCMP).rearrange("p (s h n) -> p s h n", s=TT, h=NH)
        Zc = view("f", TT * NH * NCMP).rearrange("p (s h n) -> p s h n", s=TT, h=NH)
        cneg = view("f", TT * NH * NCMP).rearrange("p (s h n) -> p s h n", s=TT, h=NH)
        c01 = view("f", TT * NH * NCMP).rearrange("p (s h n) -> p s h n", s=TT, h=NH)
        oT = view("f", 4 * T).rearrange("p (j t) -> p j t", j=4)
        grow_all = view("f", 8 * T)
        grow = grow_all.rearrange("p (m t) -> p m t", m=8)[0:MH]
        mlT = grow_all[:, 0:4 * T].rearrange("p (j t) -> p j t", j=4)
        hml = ntok[:, 0, :].rearrange("p (s e) -> p s e", s=TT)
        hsq = ntok[:, 1, :].rearrange("p (s e) -> p s e", s=TT)
        cw2 = view("f", 2 * DH).rearrange("p (v e) -> p v e", v=2)
        cw2d = view("f", P)
        hid = view("f", 2 * NG).rearrange("p (v n) -> p v n", v=2)
        htmp = view("f", 2 * NG).rearrange("p (v n) -> p v n", v=2)
        kcT = view("f", NG)
        vc = view("f", 2 * DH).rearrange("p (g e) -> p g e", g=2)
        peT = view("f", 2 * LT).rearrange("p (v i) -> p v i", v=2)
        gcol = view("f", 16).rearrange("p (a s h) -> p a s h", a=2, s=TT)
        convw = view("f", 4 * 8).rearrange("p (w m) -> p w m", w=4)
        convb = view("f", 8)
        ngc = view("f", MH)
        gb = view("f", 2)
        gn = view("f", TT * 24).rearrange("p (s n) -> p s n", s=TT)
        raw = Pb.rearrange("p z s b t -> p (z s b t)")[:, 2 * LT * 32:]
        peraw = raw[:, 0:2 * P].rearrange("p (v e) -> p v e", v=2)
        cwraw = raw[:, 2 * P:4 * P]
        craw = raw[:, 4 * P:5 * P]
        ngraw = raw[:, 5 * P:6 * P]
        gT = raw[:, 6 * P:8 * P]
        hparts = gT.rearrange("p (v e) -> p v e", v=2)
        merged = mlc
        mtmp = Pb[:, 0].rearrange("p s b t -> p (s b t)")[:, 0:512]

        rg1 = view("m", D)
        sqs = view("m", D)
        lgT = view("m", T)
        wr = view("m", KD * NE).rearrange("p (k e) -> p k e", k=KD)
        chosen = view("m", TT * TOPK * NE).rearrange("p (s j e) -> p s j e", s=TT, j=TOPK)
        logit = view("m", TT * NE).rearrange("p (s e) -> p s e", s=TT)
        memb = view("m", TT * NE).rearrange("p (s e) -> p s e", s=TT)
        rbias = view("m", NE)
        cntf = view("m", 4 * NE, 1).rearrange("p (a e) -> p a e", a=4)
        assert used["m"] <= min(16 * T, EXTRA // 2 * RW)
        used["m"] = EXTRA * RW
        rg2 = view("m", D)
        ob = view("m", TT * D)
        b1all = ob[0:NE, :]
        otmp = ob.rearrange("p (s d) -> p s d", s=TT)
        rfin = view("m", D)
        b2all = rfin[0:NE, :]
        onehot = view("m", TT * SLOTS).rearrange("p (s n) -> p s n", s=TT)
        onegate = view("m", TT * P).rearrange("p (s n) -> p s n", s=TT)
        sel_e = view("m", SLOTS, NE)
        xg = view("m", 512)
        xgT = view("m", 512).rearrange("p (m h s) -> p m h s", m=4, h=2)
        glu = view("m", 512)
        lin = view("m", 512)
        sgm = view("m", 512)
        act_t = view("m", 512)
        actT = view("m", 512).rearrange("p (m h s) -> p m h s", m=4, h=2)
        ysb = view("m", 512)
        GT = view("m", T)
        gatesT = view("m", T, NE)
        rank = view("m", TT * (NE + 1)).rearrange("p (s e) -> p s e", s=TT)
        gate = view("m", TT * NE).rearrange("p (s e) -> p s e", s=TT)
        iota_f = view("m", NBLK * 2 * SLOTS).rearrange("p (b a n) -> p b a n", b=NBLK, a=2)
        top8 = sb("top8", [P, TT, 8])
        idx8 = sb("idx8", [P, TT, 8], U32)
        idxf = sb("idxf", [P, TT, 8])
        cnt_t = sb("cnt_t", [1, NE], I32)
        next_t = sb("next_t", [1, NBLK, NE + 1], I32)
        blk_t = sb("blk_t", [1, NE + 1], I32)

        at = [0]

        def piece(n):
            at[0] += n
            return small[:, at[0] - n:at[0]]

        sqj = nT[:, :, :].rearrange("p k t -> p (k t)").rearrange("p (s d) -> p s d", s=TT)
        ssq, std, rstd = piece(TT), piece(TT), piece(TT)
        cols, csig = piece(3 * KD), piece(KD)
        ccol, g1col, g2col = (cols[:, i * KD:(i + 1) * KD] for i in range(3))
        scol, bcol = (piece(2 * KD).rearrange("p (a k) -> p a k", a=2) for _ in range(2))
        mx = piece(NH * 4).rearrange("p (h s b) -> p h s b", h=NH, s=TT)
        nmx = piece(NH * 4).rearrange("p (h s b) -> p h s b", h=NH, s=TT)
        psum_p = piece(NH * 4).rearrange("p (h s b) -> p h s b", h=NH, s=TT)
        rsc = piece(NH * 4).rearrange("p (h s b) -> p h s b", h=NH, s=TT)
        cmx = piece(TT * NH).rearrange("p (s h) -> p s h", s=TT)
        csum = piece(TT * NH).rearrange("p (s h) -> p s h", s=TT)
        den = piece(MH * TT).rearrange("p (h s) -> p h s", h=MH)
        hss = piece(TT * MH)
        hstd = piece(TT * MH)
        hr = piece(TT * MH)
        gsum = piece(TT)
        grs = piece(TT)
        gexp = piece(TT * TOPK).rearrange("p (s j) -> p s j", s=TT)
        nmax = piece(TT)

        PJ = [psum("PJ0"), psum("PJ1")]
        SC = [psum("SC0"), psum("SC1")]
        PT = [psum("PT0"), psum("PT1")]
        OB = [psum("OB0"), psum("OB1")]
        ACC = [[PT[0], PT[1]], [OB[0], OB[1]]]
        HG, HL = SC
        XB, YB = PJ

        arrived = [sem(f"arrived{i}") for i in range(RING)]
        arrived_odd = [sem(f"arrived_odd{i}") for i in range(RING)]
        ring_free = sem("ring_free")
        ada_chunk = sem("ada_chunk")
        mix_chunk = sem("mix_chunk")
        mix_tile0 = sem("mix_tile0")
        x_in = sem("x_in")
        small_in = sem("small_in")
        c_in = sem("c_in")
        turned_c = sem("turned_c")
        params_done = sem("params_done")
        gate_w_in = sem("gate_w_in")
        gate_b_in = sem("gate_b_in")
        cw2_in = sem("cw2_in")
        router_w_in = sem("router_w_in")
        adab_in = sem("adab_in")
        moe_in = sem("moe_in")
        rfin_in = sem("rfin_in")
        consts = sem("consts")
        masks = sem("masks")
        iota_made = sem("iota_made")
        pool_chain = sem("pool_chain")
        dve_chain = sem("dve_chain")
        ssq_done = [sem("ssq"), sem("ssq_second")]
        var_done = [sem("var"), sem("var_second")]
        std_done = [sem("std"), sem("std_second")]
        var_ml, std_ml = sem("var_ml"), sem("std_ml")
        turned_small = sem("turned_small")
        small_copied = sem("small_copied")
        c_exp = sem("c_exp")
        crep_done = sem("crep_done")
        mod_done = sem("mod_done")
        rows_done = sem("rows_done")
        rows_used = sem("rows_used")
        fold_made = sem("fold_made")
        gate_parts = sem("gate_parts")
        gate_parts_copied = sem("gate_parts_copied")
        mod_turned = sem("mod_turned")
        cols_done = sem("cols_done")
        ntok_done = sem("ntok_done")
        ntok_act = sem("ntok_act")
        rstd_done = sem("rstd_done")
        n_scaled = [sem("n_scaled_act"), sem("n_scaled_dve")]
        h_turned = sem("h_turned")
        logitsT_psum = sem("logitsT_psum")
        logitsT_copied = sem("logitsT_copied")
        n_turned = sem("n_turned")
        nT_copied = [sem("nT_copied0"), sem("nT_copied1")]
        proj_done = sem("proj_done")
        proj_taken = [sem("proj_taken0"), sem("proj_taken1")]
        gates_done = sem("gates_done")
        gexp_done = sem("gexp_done")
        ls_exp = sem("ls_exp")
        ls_in = sem("ls_in")
        ls_ln = sem("ls_ln")
        nm_in = sem("nm_in")
        grow_done = sem("grow_done")
        gcol_turned = sem("gcol_turned")
        gcol_done = sem("gcol_done")
        hid_done = sem("hid_done")
        hparts_copied = sem("hparts_copied")
        hid_folded = sem("hid_folded")
        gelu_in = sem("gelu_in")
        gelu_exp = sem("gelu_exp")
        hid_act = sem("hid_act")
        cmp_kv = sem("cmp_kv")
        cmp_kv_sb = sem("cmp_kv_sb")
        cmp_score = sem("cmp_score")
        cmp_sub = sem("cmp_sub")
        cmp_exp = sem("cmp_exp")
        cmp_p = sem("cmp_p")
        score_done = sem("score_done")
        max_done = sem("max_done")
        exp_done = sem("exp_done")
        probs_done = sem("probs_done")
        pt_done = sem("pt_done")
        pt_copied = [sem("pt_copied0"), sem("pt_copied1")]
        o_done = sem("o_done")
        o_copied = sem("o_copied")
        mls_done = sem("mls_done")
        mle_done = sem("mle_done")
        mpt_done = sem("mpt_done")
        num_done = sem("num_done")
        hml_done = sem("hml_done")
        hml_norm = sem("hml_norm")
        conv_done = sem("conv_done")
        conv_exp = sem("conv_exp")
        conv_act = sem("conv_act")
        mlT_turned = sem("mlT_turned")
        mlT_copied = sem("mlT_copied")
        up_done = sem("up_done")
        up_taken = sem("up_taken")
        merged_done = sem("merged_done")
        h_done = sem("h_done")
        router_done = sem("router_done")
        top_done = sem("top_done")
        top_exp = sem("top_exp")
        memb_done = sem("memb_done")
        gate_made = sem("gate_made")
        sums_begun = sem("sums_begun")
        rank_psum = sem("rank_psum")
        table_done = sem("table_done")
        gatesT_psum = sem("gatesT_psum")
        gatesT_done = sem("gatesT_done")
        hot_done = sem("hot_done")
        onegate_done = sem("onegate_done")
        gathered = sem("gathered")
        xg_copied = sem("xg_copied")
        xg_turned = sem("xg_turned")
        xgT_copied = sem("xgT_copied")
        xgT_scaled = sem("xgT_scaled")
        xg_scaled = sem("xg_scaled")
        gt_turned = sem("gt_turned")
        gt_copied = sem("gt_copied")
        biased = sem("biased")
        h_psum = sem("h_psum")
        glu_min = sem("glu_min")
        sig_glu = sem("sig_glu")
        glu_gated = sem("glu_gated")
        act_made = sem("act_made")
        act_turned = sem("act_turned")
        actT_copied = sem("actT_copied")
        y_psum = sem("y_psum")
        y_copied = sem("y_copied")
        added = sem("added")
        final_done = sem("final_done")
        out_done = sem("out_done")

        block = ctx.enter_context(nc.Block())

        freed, n_proj, n_ada = {}, 0, 0
        for item in order:
            if item[0] == "proj":
                n_proj += 1
                freed[item] = (proj_done, n_proj)
            elif item[0] == "ada":
                n_ada += 1
                freed[item] = (ada_chunk, n_ada)
            elif item[0] == "compress":
                freed[item] = (hid_done, item[1] + 1)
            elif item[0] == "up":
                freed[item] = (up_done, 4 * (item[1] + 1))
            else:
                freed[item] = (mix_chunk, item[1] + 1)
        owner = {}
        for item in order:
            s, n, at_, _ = loads[item]
            for a in range(n):
                owner[at_ + a] = item

        def owners_before(at_, n):
            found = []
            for a in range(at_, at_ + n):
                back = a - RING
                while back >= first and back not in owner:
                    back -= RING
                if back >= first and freed[owner[back]] not in found:
                    found.append(freed[owner[back]])
            return found

        def arrive(eng, item):
            s, _, _, count = loads[item]
            eng.wait_ge(arrived[s], count)

        def ring_k(item):
            return ring[:, loads[item][0], :].rearrange("p (k n) -> p k n", k=KD)

        def each_block(eng, body):
            with eng.Fori(0, NE) as e:
                cnt = eng.value_load(cnt_t[0:1, bass.ds(e, 1)], min_val=0, max_val=T)
                before = eng.value_load(blk_t[0:1, bass.ds(e, 1)], min_val=0, max_val=NBLK * NE)
                num = eng.value_load(blk_t[0:1, bass.ds(e + 1, 1)], min_val=1, max_val=NBLK * NE)
                for b in range(1, NBLK):
                    with eng.If(cnt > SLOTS * b):
                        body(e, before + b, b, False)
                body(e, num, 0, True)

        def slot_of(e, ch):
            return (PER_E * e + ch) % SPAN

        @block.sync
        def _(sp):
            def expert_chunk(e, e_mod, ch):
                slot = slot_of(e_mod, ch)
                if ch < KD:
                    src = exp_w1[bass.ds(e, 1), ch * P:(ch + 1) * P, :].rearrange("a p n -> p a n")
                    dst = ring[:, slot:slot + 1, :]
                else:
                    r0 = (ch - KD) * 2 * P
                    src = exp_w2[bass.ds(e, 1), r0:r0 + 2 * P, :].rearrange("a (k p) n -> p (a k) n", p=P)
                    dst = ring[:, slot, :].rearrange("p (k n) -> p k n", n=D)
                sp.dma_start(dst, src).then_inc((arrived, arrived_odd)[e_mod % 2][ch], 16)

            sp.dma_start(craw[0:KD, :], c.rearrange("a (k p) -> (a k) p", p=P)).then_inc(c_in, 16)
            for item in order:
                kind = item[0]
                if item == ("ada", 0, 3):
                    sp.dma_start(xres[:], x.rearrange("(s p) d -> p s d", p=P)).then_inc(x_in, 16)
                    for v, pe_ in enumerate((pe_k, pe_v)):
                        sp.dma_start(peraw[0:LT, v, :], pe_.rearrange("(i a) e -> i (a e)", a=2)).then_inc(small_in, 16)
                    sp.dma_start(cwraw[0:32, 0:P], conv_w.rearrange("w (m p) -> (w m) p", p=P)).then_inc(small_in, 16)
                    sp.dma_start(cwraw[0:8, P:2 * P], conv_b.rearrange("(m p) -> m p", p=P)).then_inc(small_in, 16)
                    sp.dma_start(ngraw[0:MH, :], norm_g.rearrange("(h p) -> h p", p=P)).then_inc(small_in, 16)
                s, n, at_, _ = loads[item]
                for event, value in owners_before(at_, n):
                    sp.wait_ge(event, value)
                if kind == "ada":
                    _, p, k = item
                    sp.dma_start(ring[:, s, :], ada_w[k * P:(k + 1) * P, p * RW:(p + 1) * RW]).then_inc(arrived[s], 16)
                elif kind == "proj" and item[1] < C_KV:
                    dst = ring_k(item).rearrange("p k (r g d) -> p k r g d", r=2, g=2)
                    for r in range(2):
                        for g in range(2):
                            a = item[1] // 2 + (g * NR + r) * DH
                            sp.dma_start(dst[:, :, r, g, :], w_in[:, a:a + DH].rearrange("(k p) n -> p k n", p=P)
                                         ).then_inc(arrived[s], 16)
                elif kind == "proj":
                    sp.dma_start(ring_k(item), w_in[:, item[1]:item[1] + 256].rearrange("(k p) n -> p k n", p=P)
                                 ).then_inc(arrived[s], 16)
                elif kind == "compress":
                    sp.dma_start(ring[:, s, :].rearrange("p (i n) -> p i n", i=LT),
                                 (cw1_k, cw1_v)[item[1]].rearrange("(i p) n -> p i n", p=P)).then_inc(arrived[s], 16)
                elif kind == "up":
                    sp.dma_start(ring[:, s:s + 2, :].rearrange("p a (k n) -> p (a k) n", n=D),
                                 (w_up_nsa, w_up_ml)[item[1]].rearrange("(k p) n -> p k n", p=P)).then_inc(arrived[s], 16)
                else:
                    i = item[1]
                    sp.dma_start(ring[:, s, :].rearrange("p (k n) -> p k n", n=D),
                                 w_out[2 * i * P:2 * (i + 1) * P, :].rearrange("(k p) n -> p k n", p=P)
                                 ).then_inc(arrived[s], 16)
            for ch in range(PER_E):
                for event, value in owners_before(MOE0 + ch, 1):
                    sp.wait_ge(event, value)
                expert_chunk(0, 0, ch)
            sp.wait_ge(mix_chunk, KD // 2)
            for ch in range(EXTRA // 2, EXTRA):
                expert_chunk(1, 1, ch)
            sp.wait_ge(table_done, 1)
            for ch in range(EXTRA // 2):
                expert_chunk(1, 1, ch)

            def later_chunks(e, e_mod, chunks, after):
                prev = sp.value_load(blk_t[0:1, bass.ds(e, 1)], min_val=1, max_val=NBLK * NE)
                for ch in chunks:
                    old = ch + PER_E * (after + 1) - SPAN
                    if old == KD - 1:
                        sp.wait_ge(h_psum, prev)
                    elif old == PER_E - 1:
                        sp.wait_ge(y_psum, prev)
                    else:
                        sp.wait_ge(ring_free, e * (PER_E - 2) + ((old if old >= KD else old + 1) - (PER_E - 2)))
                    expert_chunk(e + after, e_mod + after, ch)

            with sp.Fori(0, NE // TURN - 1) as turn:
                for j in range(1, TURN + 1):
                    later_chunks(turn * TURN + j, j, range(EXTRA, PER_E), 0)
                    later_chunks(turn * TURN + j, j, range(EXTRA), 1)
            for e in range(NE - TURN + 1, NE):
                later_chunks(e, e % TURN, range(EXTRA, PER_E), 0)
                if e < NE - 1:
                    later_chunks(e, e % TURN, range(EXTRA), 1)
            for s in range(TT):
                sp.wait_ge(final_done, s + 1)
                sp.dma_start(out[s * P:(s + 1) * P, :], otmp[:, s, :]).then_inc(out_done, 16)
            sp.wait_ge(out_done, 16 * TT)

        @block.gpsimd
        def _(pool):
            chain = [0]

            def link(ins):
                chain[0] += 1
                ins.then_inc(pool_chain, 1)
                pool.wait_ge(pool_chain, chain[0])

            made = {}

            def step(ins, signal):
                made[signal.name] = made.get(signal.name, 0) + 1
                ins.then_inc(signal, 1)
                pool.wait_ge(signal, made[signal.name])

            link(pool.memset(ident[:], 0.0))
            link(pool.affine_select(out=ident[:], in_=ident[:], compare_op=ALU.not_equal, fill=1.0,
                                    base=0, pattern=[[-1, P]], channel_multiplier=1))
            step(pool.tensor_copy(identb[:], ident[:]), consts)
            link(pool.memset(sel0[:], 0.0))
            for j in range(4):
                ins = pool.memset(sel0[32 * j:32 * j + 1, :], 1.0)
                if j < 3:
                    link(ins)
            step(ins, consts)
            step(pool.memset(ones[:], 1.0), consts)
            for v, w2_ in enumerate((cw2_k, cw2_v)):
                pool.dma_start(cw2[:, v, :], w2_).then_inc(cw2_in, 16)
            link(pool.memset(cmaskb[:], 0.0))
            step(pool.affine_select(out=cmaskb[:], in_=cmaskb[:], compare_op=ALU.is_ge, fill=-1e30,
                               base=0, pattern=[[-1, P]], channel_multiplier=1), masks)
            link(pool.memset(tmaskb[:], 0.0))
            step(pool.affine_select(out=tmaskb[:], in_=tmaskb[:], compare_op=ALU.is_ge, fill=1e30,
                               base=0, pattern=[[1, P]], channel_multiplier=-1), masks)
            link(pool.memset(lower[:], 1.0))
            step(pool.affine_select(out=lower[:], in_=lower[:], compare_op=ALU.is_gt, fill=0.0,
                               base=0, pattern=[[1, P]], channel_multiplier=-1), masks)
            link(pool.memset(sel4[:], 1.0))
            step(pool.affine_select(out=sel4[:], in_=sel4[:], compare_op=ALU.is_equal, fill=0.0,
                               base=0, pattern=[[1, MH], [0, P]], channel_multiplier=-1), masks)
            link(pool.memset(cneg, 0.0))
            link(pool.memset(c01, 1.0))
            for m, f in ((cneg, -1e30), (c01, 0.0)):
                for s in range(TT):
                    step(pool.affine_select(out=m[:, s], in_=m[:, s], compare_op=ALU.is_ge, fill=f,
                                       base=s * P - (CLEN - 1), pattern=[[0, NH], [-STRIDE, NCMP]],
                                       channel_multiplier=1), masks)
            step(pool.memset(mlx[:, :, 0:3], 0.0), masks)
            step(pool.memset(mlv[:, :, :, 128:129], 1.0), masks)
            step(pool.memset(kpe[:, :, :, NG:], 0.0), masks)
            pool.wait_ge(ada_chunk, KD - 1)
            with nc.allow_non_contiguous_dma(reason="eight words"):
                pool.dma_start(gb[0:MH, :], gate_b.rearrange("(a h) -> h a", a=2)).then_inc(gate_b_in, 16)
            with nc.allow_non_contiguous_dma(reason="gate columns"):
                pool.dma_start(wgate[:, :, 0:24], w_in[:, C_NG:C_NG + 24].rearrange("(k p) n -> p k n", p=P)).then_inc(gate_w_in, 16)
                pool.dma_start(wgate[:, :, 24:32], w_in[:, C_IF:C_IF + 8].rearrange("(k p) n -> p k n", p=P)).then_inc(gate_w_in, 16)
            pool.wait_ge(merged_done, 1)
            pool.iota(iota_f, pattern=[[SLOTS, NBLK], [0, 2], [1, SLOTS]], base=0, channel_multiplier=0,
                      allow_small_or_imprecise_dtypes=True).then_inc(iota_made, 1)
            pool.dma_start(wr, router_w.rearrange("(k p) n -> p k n", p=P)).then_inc(router_w_in, 16)
            pool.dma_start(b1all, exp_b1).then_inc(moe_in, 16)
            pool.dma_start(b2all, exp_b2).then_inc(moe_in, 16)
            pool.dma_start(rbias, router_b.rearrange("(a d) -> a d", a=1).to_broadcast([P, NE])).then_inc(moe_in, 16)
            pool.wait_ge(sums_begun, 1)
            pool.dma_start(rfin, final_g.rearrange("(a d) -> a d", a=1).to_broadcast([P, D])).then_inc(rfin_in, 16)
        @block.tensor
        def _(pe):
            mm, tr = pe.matmul, pe.transpose
            state = {"proj": 0}

            def proj_bank():
                b, n = state["proj"] % 2, state["proj"] // 2
                if n:
                    pe.wait_ge(proj_taken[b], n)
                state["proj"] += 1
                return PJ[b]

            def t_tile(bank, col, w, n0):
                for k in range(KD):
                    last = mm(bank[:, col:col + T], w[:, k, n0:n0 + P], nT[:, k, :],
                              start=(k == 0), stop=(k == KD - 1), skip_group_check=True)
                return last

            def tok_tile(bank, col, w, n0, n, s):
                for k in range(KD):
                    last = mm(bank[:, col:col + n], nT[:, k, s * P:(s + 1) * P], w[:, k, n0:n0 + n],
                              start=(k == 0), stop=(k == KD - 1), skip_group_check=True)
                return last

            def project(item):
                arrive(pe, item)
                if state["proj"] == 0:
                    for n_ in range(2):
                        pe.wait_ge(nT_copied[n_], 2)
                        pe.wait_ge(n_scaled[n_], 1)
                bank, w, col = proj_bank(), ring_k(item), item[1]
                if col in (C_KV + 256, C_KV + 512):
                    t_tile(bank, 0, w, 0)
                    tok_tile(bank, T, w, P, P, 0)
                    last = tok_tile(bank, T + P, w, P, P, 1)
                elif C_V <= col < C_MG:
                    tok_tile(bank, 0, w, 0, T, 0)
                    last = tok_tile(bank, T, w, 0, T, 1)
                else:
                    t_tile(bank, 0, w, 0)
                    last = t_tile(bank, T, w, P)
                last.then_inc(proj_done, 1)

            def small_rows():
                pe.wait_ge(consts, 3)
                pe.wait_ge(c_in, 16 * 3)
                tr(SC[0][:, 0:3 * KD], craw[0:3 * KD, :], ident[0:3 * KD, 0:3 * KD]).then_inc(turned_c, 1)

            def params():
                pe.wait_ge(small_in, SMALL)
                for v in range(2):
                    tr(OB[1][:, 16 + LT * v:16 + LT * (v + 1)], peraw[0:LT, v, :], ident[0:LT, 0:LT])
                tr(OB[1][:, 64:96], cwraw[0:32, 0:P], ident[0:32, 0:32])
                tr(OB[1][:, 96:104], cwraw[0:8, P:2 * P], ident[0:8, 0:8])
                tr(OB[1][:, 104:108], ngraw[0:MH, :], ident[0:MH, 0:MH]).then_inc(turned_small, 1)

            def ada(item):
                _, p, k = item
                if p == 0 and k == 0:
                    pe.wait_ge(crep_done, 1)
                if p == 1 and k == 0:
                    pe.wait_ge(params_done, 1)
                if p == 2 and k == 0:
                    pe.wait_ge(mod_done, 2)
                arrive(pe, item)
                bank = OB[min(p, 1)]
                for j in range(4):
                    last = mm(bank[32 * j:32 * j + 32, :], crep[:, k, :],
                              ring[:, loads[item][0], j * 512:(j + 1) * 512],
                              start=(k == 0), stop=(k == KD - 1), tile_position=(0, 32 * j), skip_group_check=True)
                last.then_inc(ada_chunk, 1)

            def spread(bank, p, j):
                return mm(bank[:, :], sel0[32 * j:32 * j + 32, :], modrow[32 * j:32 * j + 32, p, :],
                          start=True, stop=True, tile_position=(32 * j, 0))

            def mod_cols(i):
                if i == 0:
                    pe.wait_ge(mod_done, 1)
                    parts = ((0, SC[0]),)
                else:
                    pe.wait_ge(mod_done, 3)
                    parts = ((1, SC[0]), (2, SC[1]))
                for p, bank in parts:
                    for c_ in range(4):
                        last = tr(bank[:, c_ * P:(c_ + 1) * P], modrow[:, p, c_ * P:(c_ + 1) * P], ident[:, :])
                last.then_inc(mod_turned, 1)

            def turn_n():
                pe.wait_ge(ntok_done, 1)
                for q in range(4):
                    if q >= 2:
                        pe.wait_ge(nT_copied[q % 2], q // 2)
                    for a in range(2):
                        for s in range(TT):
                            k = 2 * q + a
                            last = tr(PJ[q % 2][:, a * T + s * P:a * T + (s + 1) * P],
                                      ntok[:, s, k * P:(k + 1) * P], ident[:, :])
                    last.then_inc(n_turned, 1)

            def compress(item):
                v = item[1]
                arrive(pe, item)
                if v == 0:
                    pe.wait_ge(proj_taken[0], 1)
                    pe.wait_ge(masks, MASKS)
                w = ring[:, loads[item][0], :].rearrange("p (i n) -> p i n", i=LT)
                for i in range(LT):
                    j = i % 4
                    last = mm(PT[v][32 * j:32 * j + 32, 0:P], kpe[:, v, i, :], w[:, i, :], start=(i < 4),
                              stop=(i >= LT - 4), tile_position=(0, 32 * j), skip_group_check=True)
                last.then_inc(hid_done, 1)

            def cmp_fold():
                pe.wait_ge(hparts_copied, 1)
                for v in range(2):
                    last = mm(PT[v][:, P:P + NG], hparts[:, v, :], fold[:, 0:NG], start=True, stop=True,
                              skip_group_check=True)
                last.then_inc(hid_folded, 1)

            def gate_sums():
                pe.wait_ge(mod_done, 1)
                pe.wait_ge(gate_w_in, 16 * 2)
                for k in range(KD):
                    j = k % 4
                    last = mm(OB[0][32 * j:32 * j + 32, 0:T], wgate[:, k, :], nT[:, k, :],
                              start=(k < 4), stop=(k >= 4), tile_position=(0, 32 * j), skip_group_check=True)
                last.then_inc(gate_parts, 1)

            def gates():
                pe.wait_ge(gate_parts_copied, 1)
                for s in range(TT):
                    mm(OB[0][:, 24 * s:24 * s + 24], gT[:, s * P:(s + 1) * P], fold[:, 0:24],
                       start=True, stop=True, skip_group_check=True)
                for a in range(2):
                    last = mm((OB[0], SC[0])[a][0:MH, 64:64 + T], fold[:, 24 + MH * a:24 + MH * (a + 1)], gT,
                              start=True, stop=True, skip_group_check=True)
                last.then_inc(gates_done, 1)

            def gate_cols():
                pe.wait_ge(grow_done, 1)
                for a in range(2):
                    for s in range(TT):
                        last = tr(SC[1][:, 8 * a + 4 * s:8 * a + 4 * s + 4],
                                  grow[:, 5 + a, s * P:(s + 1) * P], ident[0:MH, 0:MH])
                last.then_inc(gcol_turned, 1)

            def cmp_keys():
                pe.wait_ge(hid_act, 1)
                mm(PT[0][:, 64:64 + NG], cw2d, hid[:, 0, :], start=True, stop=True)
                for g in range(2):
                    last = mm(PT[0][0:NCMP, 128 + DH * g:128 + DH * (g + 1)], hid[:, 1, g * NCMP:(g + 1) * NCMP],
                              cw2[:, 1, :], start=True, stop=True)
                last.then_inc(cmp_kv, 1)

            def cmp_scores():
                pe.wait_ge(cmp_kv_sb, 1)
                pe.wait_ge(gexp_done, 1)
                pe.wait_ge(grow_done, 1)
                for s in range(TT):
                    for r, g in ((r, g) for r in range(NR) for g in range(2)):
                        o = (s * NR + r) * NCMP
                        last = mm((OB[0], SC[0])[g][:, o:o + NCMP], qT[64 * g:64 * g + 64, r, s * P:(s + 1) * P],
                                  kcT[64 * g:64 * g + 64, g * NCMP:(g + 1) * NCMP], start=True, stop=True,
                                  skip_group_check=True)
                last.then_inc(cmp_score, 1)

            def head_scores(h):
                g, r = divmod(h, NR)
                if h == 0:
                    pe.wait_ge(masks, MASKS)
                    pe.wait_ge(gcol_done, 1)
                    pe.wait_ge(cmp_sub, 1)
                else:
                    pe.wait_ge(exp_done, h)
                for s in range(TT):
                    n = (s + 1) * P
                    for b in range(2):
                        mm(SC[s][:, b * T:b * T + n], qT[64 * g:64 * g + 64, r, s * P:(s + 1) * P],
                           kT[64 * g:64 * g + 64, b, 0:n], start=True, stop=False, skip_group_check=True)
                        last = mm(SC[s][:, b * T + s * P:b * T + n], identb[:, :], cmaskb[:, :],
                                  start=False, stop=True, skip_group_check=True)
                last.then_inc(score_done, 1)

            def head_turn(h):
                pe.wait_ge(probs_done, h + 1)
                if h == 0:
                    pe.wait_ge(cmp_p, 1)
                for b in range(2):
                    for n, (s_, t_) in enumerate(((0, 0), (0, 1), (1, 1))):
                        tr(PT[b][:, n * P:(n + 1) * P], Pb[:, h % 2, t_, b, s_ * P:(s_ + 1) * P], ident[:, :])
                    last = tr(PT[b][0:NCMP, 384:512], Pc[:, b, h, :], ident[:, :])
                last.then_inc(pt_done, 1)

            def head_out(h):
                g = h // NR
                j, half = divmod(h, 2)
                o = OB[0][64 * half:64 * half + 64, :]
                at = (0, 64 * half)
                pe.wait_ge(pt_copied[0], h + 1)
                pe.wait_ge(pt_copied[1], h + 1)
                if half == 0 and j:
                    pe.wait_ge(o_copied, j)
                for b in range(2):
                    mm(o[:, 0:T], vS[:, 0, b, 64 * g:64 * g + 64], PTb[:, b, 0:T],
                       start=(b == 0), stop=False, tile_position=at, skip_group_check=True)
                    mm(o[:, P:T], vS[:, 1, b, 64 * g:64 * g + 64], PTb[:, b, T:T + P],
                       start=False, stop=False, tile_position=at, skip_group_check=True)
                mm(o[:, 0:T], vc[0:NCMP, g, :], PcT[0:NCMP, :],
                   start=False, stop=True, tile_position=at, skip_group_check=True).then_inc(o_done, 1)

            def ml_scores(m):
                if m == 0:
                    pe.wait_ge(conv_act, 4)
                    pe.wait_ge(exp_done, NH)
                for s in range(TT):
                    n = T - s * P
                    mm(SC[s][:, 0:n], sel4[:, m, :], grow[:, 4, s * P:T], start=True, stop=False, skip_group_check=True)
                    mm(SC[s][:, 0:P], identb[:, :], tmaskb[:, :], start=False, stop=True, skip_group_check=True)
                    last = mm(SC[s][:, T:T + n], mlc[:, MH + m, s * P:(s + 1) * P], mlc[:, m, s * P:T],
                              start=True, stop=True, skip_group_check=True)
                last.then_inc(mls_done, 1)

            def ml_out(m):
                pe.wait_ge(mpt_done, m + 1)
                if m:
                    pe.wait_ge(hml_done, m)
                mm(PT[0][:, 0:129], MPT[:, 0:P], mlv[:, 0, m, :], start=True, stop=True, skip_group_check=True)
                mm(PT[0][:, 129:258], MPT[:, P:2 * P], mlv[:, 0, m, :], start=True, stop=False, skip_group_check=True)
                mm(PT[0][:, 129:258], MPT[:, 2 * P:3 * P], mlv[:, 1, m, :],
                   start=False, stop=True, skip_group_check=True).then_inc(num_done, 1)

            def ml_turn():
                pe.wait_ge(hml_norm, 1)
                for m in range(MH):
                    for s in range(TT):
                        last = tr(SC[m // 2][:, (m % 2) * T + s * P:(m % 2) * T + (s + 1) * P],
                                  hml[:, s, m * P:(m + 1) * P], ident[:, :])
                last.then_inc(mlT_turned, 1)

            def up(item):
                a = item[1]
                arrive(pe, item)
                if a == 0:
                    pe.wait_ge(o_copied, 4)
                    for b in range(2):
                        pe.wait_ge(proj_taken[b], (n_proj + 1 - b) // 2)
                else:
                    pe.wait_ge(mlT_copied, MH)
                s0 = loads[item][0]
                w = ring[:, s0:s0 + 2, :].rearrange("p a (k n) -> p (a k) n", n=D)
                src = (oT, mlT)[a]
                for q in range(4):
                    if a or q >= 2:
                        pe.wait_ge(up_taken, 4 * a + q - 1)
                    for i in range(2):
                        for k in range(4):
                            last = mm(PJ[q % 2][:, i * T:(i + 1) * T], w[:, k, (2 * q + i) * P:(2 * q + i + 1) * P],
                                      src[:, k, :], start=(k == 0), stop=(k == 3), skip_group_check=True)
                    last.then_inc(up_done, 1)

            def gate_rows(i):
                if i == 0:
                    pe.wait_ge(mod_done, 2)
                    pe.wait_ge(hml_done, MH)
                    for half in range(2):
                        last = spread(PT[half], 1, half)
                else:
                    pe.wait_ge(h_done, 1)
                    for half in range(2):
                        last = spread(OB[half], 2, 2 + half)
                last.then_inc(rows_done, 1)

            def mix(i, s):
                w = ring[:, loads[("mix", i)][0], :].rearrange("p (k n) -> p k n", n=D)
                for kk in range(2):
                    k = 2 * i + kk
                    for half in range(2):
                        last = mm((OB, PJ)[s][half][:, :], merged[:, k, s * P:(s + 1) * P],
                                  w[:, kk, half * HD:(half + 1) * HD],
                                  start=(k == 0), stop=(k == KD - 1), skip_group_check=True)
                if s == 0 and i == KD // 2 - 1:
                    last.then_inc(mix_tile0, 1)
                if s == 1:
                    last.then_inc(mix_chunk, 1)

            def second_norm(s):
                pe.wait_ge(ntok_done, 2 + s)
                pe.wait_ge(ntok_act, 1 + s)
                pe.wait_ge(cols_done, 2)
                if s:
                    for n_ in range(2):
                        pe.wait_ge(n_scaled[n_], 2)
                for k in range(KD):
                    last = tr(SC[k // 4][:, (k % 4) * P:(k % 4 + 1) * P], ntok[:, s, k * P:(k + 1) * P], ident[:, :])
                last.then_inc(h_turned, 1)

            def logits(s):
                for n_ in range(2):
                    pe.wait_ge(n_scaled[n_], 2 + s)
                if s == 0:
                    pe.wait_ge(router_w_in, 16)
                    pe.wait_ge(rows_used, 1)
                for k in range(KD):
                    j = k % 4
                    last = mm(PT[0][32 * j:32 * j + 32, s * P:(s + 1) * P], wr[:, k, :], nT[:, k, s * P:(s + 1) * P],
                              start=(k < 4), stop=(k >= 4), tile_position=(0, 32 * j), skip_group_check=True)
                last.then_inc(logitsT_psum, 1)
                pe.wait_ge(logitsT_copied, s + 1)
                last = tr(PT[1][:, s * P:(s + 1) * P], lgT[:, s * P:(s + 1) * P], ident[:, :])
                if s:
                    last.then_inc(router_done, 1)

            def router():
                pe.wait_ge(memb_done, 1)
                mm(PT[0][:, 0:NE], lower[:, :], memb[:, 0, :], start=True, stop=True, skip_group_check=True)
                mm(PT[0][:, NE:2 * NE], ones[:, :], memb[:, 0, :], start=True, stop=False, skip_group_check=True)
                mm(PT[0][:, NE:2 * NE], lower[:, :], memb[:, 1, :], start=False, stop=True, skip_group_check=True)
                mm(PT[0][0:1, 64:64 + NE], ones[:, 0:1], memb[:, 0, :], start=True, stop=False, skip_group_check=True)
                mm(PT[0][0:1, 64:64 + NE], ones[:, 0:1], memb[:, 1, :],
                   start=False, stop=True, skip_group_check=True).then_inc(rank_psum, 1)
                pe.wait_ge(gate_made, 1)
                for s in range(TT):
                    last = tr(XB[0:NE, s * P:(s + 1) * P], gate[:, s, :], ident[:, :])
                last.then_inc(gatesT_psum, 1)

            def init_sums():
                pe.wait_ge(moe_in, 16 * 3)
                pe.wait_ge(rows_used, 2)
                for s in range(TT):
                    for half in range(2):
                        last = mm(ACC[s][half][:, :], gatesT[:, s * P:(s + 1) * P], b2all[:, half * HD:(half + 1) * HD],
                                  start=True, stop=False, skip_group_check=True)
                last.then_inc(sums_begun, 1)

            for item in sched:
                kind = item[0]
                if kind == "small":
                    small_rows()
                elif kind == "params":
                    params()
                elif kind == "ada":
                    ada(item)
                elif kind == "mod_cols":
                    mod_cols(item[1])
                elif kind == "turn":
                    turn_n()
                elif kind == "proj":
                    project(item)
                elif kind == "gate_sums":
                    gate_sums()
                elif kind == "gates":
                    gates()
                elif kind == "compress":
                    compress(item)
                elif kind == "cmp_fold":
                    cmp_fold()
                elif kind == "gate_cols":
                    gate_cols()
                elif kind == "cmp_keys":
                    cmp_keys()
                elif kind == "cmp_scores":
                    cmp_scores()
                elif kind == "head_scores":
                    head_scores(item[1])
                elif kind == "head_turn":
                    head_turn(item[1])
                elif kind == "head_out":
                    head_out(item[1])
                elif kind == "ml_scores":
                    ml_scores(item[1])
                elif kind == "ml_out":
                    ml_out(item[1])
                elif kind == "ml_turn":
                    ml_turn()
                elif kind == "up":
                    up(item)
                elif kind == "gate_rows":
                    gate_rows(item[1])
                elif kind == "mix":
                    arrive(pe, item)
                    if item[1] == 0:
                        pe.wait_ge(merged_done, 1)
                    mix(item[1], 0)
                elif kind == "mix_tile":
                    for i in range(2 * item[2], 2 * item[2] + 2):
                        mix(i, 1)
                elif kind == "second_norm":
                    second_norm(item[1])
                elif kind == "logits":
                    logits(item[1])
                elif kind == "router":
                    router()

            def gather(num):
                pe.wait_ge(hot_done, num)
                for s in range(TT):
                    for half in range(2):
                        last = mm(XB[64 * half:64 * half + 64, :], onehot[:, s, :],
                                  ntok[:, s, half * HD:(half + 1) * HD],
                                  start=(s == 0), stop=(s == TT - 1), tile_position=(0, 64 * half),
                                  skip_group_check=True)
                last.then_inc(gathered, 1)

            def turn_gathered():
                for m in range(4):
                    last = tr(YB[:, m * P:(m + 1) * P], xg[:, m * P:(m + 1) * P], ident[:, :])
                last.then_inc(xg_turned, 1)

            def bias():
                for q, bank in enumerate((HG, HL)):
                    for half in range(2):
                        last = mm(bank[64 * half:64 * half + 64, :], sel_e[:, :],
                                  b1all[:, q * D + half * HD:q * D + (half + 1) * HD],
                                  start=True, stop=False, tile_position=(0, 64 * half), skip_group_check=True)
                last.then_inc(biased, 1)

            def add_block(tiles):
                for s in tiles:
                    for half in range(2):
                        last = mm(ACC[s][half][:, :], GT[64 * half:64 * half + 64, s * P:(s + 1) * P],
                                  ysb[64 * half:64 * half + 64, :], start=False, stop=False,
                                  tile_position=(64 * half, 0), skip_group_check=True)
                return last

            pe.wait_ge(moe_in, 16 * 3)
            bias()
            pe.wait_ge(gatesT_done, 1)
            gather(1)
            pe.wait_ge(xg_copied, 1)
            turn_gathered()

            def expert_block(turn, e_mod, num, main):
                pe.wait_ge(xgT_scaled, num)

                def chunk_arrived(ch):
                    seen = (e_mod // 2 + 1) * 16 + (0 if e_mod % 2 else per_slot[ch])
                    pe.wait_ge((arrived, arrived_odd)[e_mod % 2][ch], turn * (TURN // 2 * 16) + seen)

                def weights(ch, lo, hi):
                    return ring[:, slot_of(e_mod, ch), lo:hi]

                for k in range(KD):
                    chunk_arrived(k)
                    for q, bank in enumerate((HG, HL)):
                        for half in range(2):
                            last = mm(bank[64 * half:64 * half + 64, :], xgT[:, k % 4, k // 4, :],
                                      weights(k, q * D + half * HD, q * D + (half + 1) * HD),
                                      start=False, stop=(k == KD - 1), tile_position=(0, 64 * half),
                                      skip_group_check=True)
                    if k == KD - 1:
                        last.then_inc(h_psum, 1)
                    elif main:
                        last.then_inc(ring_free, 1)
                gather(num + 1)
                with pe.If(num < 2):
                    init_sums()
                with pe.If(num > 1):
                    pe.wait_ge(y_copied, num)
                    pe.wait_ge(gt_copied, num)
                    add_block(range(TT))
                pe.wait_ge(onegate_done, num)
                for s in range(TT):
                    last = tr(YB[:, s * P:(s + 1) * P], onegate[:, s, :], ident[:, :])
                last.then_inc(gt_turned, 1)
                pe.wait_ge(act_made, num)
                pe.wait_ge(xg_copied, num + 1)
                for m in range(4):
                    last = tr(XB[:, m * P:(m + 1) * P], act_t[:, m * P:(m + 1) * P], ident[:, :])
                last.then_inc(act_turned, 1)
                pe.wait_ge(gt_copied, num + 1)
                turn_gathered()
                bias()
                pe.wait_ge(actT_copied, num)
                pe.wait_ge(xgT_copied, num + 1)
                for k in range(KD):
                    ch = KD + k // 2
                    if k % 2 == 0:
                        chunk_arrived(ch)
                    for half in range(2):
                        last = mm(YB[64 * half:64 * half + 64, :], actT[:, k % 4, k // 4, :],
                                  weights(ch, (k % 2) * D + half * HD, (k % 2) * D + (half + 1) * HD),
                                  start=(k == 0), stop=(k == KD - 1), tile_position=(0, 64 * half),
                                  skip_group_check=True)
                    if k % 2 == 1 and k < KD - 1 and main:
                        last.then_inc(ring_free, 1)
                last.then_inc(y_psum, 1)

            pe.wait_ge(table_done, 1)
            with pe.Fori(0, NE // TURN) as turn:
                for j in range(TURN):
                    cnt = pe.value_load(cnt_t[0:1, bass.ds(turn * TURN + j, 1)], min_val=0, max_val=T)
                    before = pe.value_load(blk_t[0:1, bass.ds(turn * TURN + j, 1)], min_val=0, max_val=NBLK * NE)
                    num = pe.value_load(blk_t[0:1, bass.ds(turn * TURN + (j + 1), 1)], min_val=1, max_val=NBLK * NE)
                    with pe.If(cnt > SLOTS):
                        with pe.Fori(1, NBLK) as b:
                            with pe.If(cnt > b * SLOTS):
                                expert_block(turn, j, before + b, False)
                    expert_block(turn, j, num, True)
            total = pe.value_load(blk_t[0:1, NE:NE + 1], min_val=1, max_val=NBLK * NE)
            pe.wait_ge(y_copied, total + 1)
            pe.wait_ge(gt_copied, total + 1)
            for s in range(TT):
                add_block((s,)).then_inc(added, 1)

        @block.scalar
        def _(act):
            A = act.activation
            state = {"proj": 0}

            for i, g_ in enumerate((norm1_g, norm2_g)):
                act.dma_start(craw[(i + 1) * KD:(i + 2) * KD, :], g_.rearrange("(k p) -> k p", p=P)).then_inc(c_in, 16)
            for j in range(4):
                act.dma_start(modrow[32 * j:32 * j + 32, :, :],
                              ada_b.rearrange("(a p j n) -> a p j n", a=1, p=3, j=4)[:, :, j, :].to_broadcast([32, 3, 512])
                              ).then_inc(adab_in, 16)

            def taken():
                b = state["proj"] % 2
                state["proj"] += 1
                return proj_taken[b]

            for item in sched:
                kind = item[0]
                if kind == "small":
                    act.wait_ge(small_copied, 1)
                    A(csig, ccol, ACT.Tanh, scale=0.5).then_inc(c_exp, 1)
                elif kind == "norm":
                    act.wait_ge(x_in, 16)
                    for s in range(TT):
                        last = A(sqj[:, s, :], xres[:, s, :], ACT.Square, accum_out=ssq[:, s:s + 1])
                    last.then_inc(ssq_done[0], 1)
                    act.wait_ge(var_done[0], 1)
                    A(std, ssq, ACT.Sqrt).then_inc(std_done[0], 1)
                elif kind == "turn":
                    for q in (0, 2):
                        act.wait_ge(n_turned, q + 1)
                        A(nT[:, 2 * q:2 * q + 2, :], PJ[0].rearrange("p (a t) -> p a t", a=2), ACT.Copy
                          ).then_inc(nT_copied[0], 1)
                elif kind == "mod_cols" and item[1] == 0:
                    act.wait_ge(cols_done, 1)
                    for q in (0, 2):
                        act.wait_ge(nT_copied[0], q // 2 + 1)
                        for k in (2 * q, 2 * q + 1):
                            last = A(nT[:, k, :], nT[:, k, :], ACT.Identity, bias=bcol[:, 0, k:k + 1], scale=scol[:, 0, k:k + 1])
                    last.then_inc(n_scaled[0], 1)
                elif kind == "second_norm":
                    s = item[1]
                    act.wait_ge(h_done, s + 1)
                    A(sqs, xres[:, s, :], ACT.Square, accum_out=ssq[:, s:s + 1]).then_inc(ssq_done[1], 1)
                    act.wait_ge(var_done[1], s + 1)
                    A(std[:, s:s + 1], ssq[:, s:s + 1], ACT.Sqrt).then_inc(std_done[1], 1)
                    act.wait_ge(rstd_done, s + 1)
                    A(ntok[:, s, HD:], xres[:, s, HD:], ACT.Copy, scale=rstd[:, s:s + 1]).then_inc(ntok_act, 1)
                    act.wait_ge(h_turned, s + 1)
                    for k in range(4):
                        last = A(nT[:, k, s * P:(s + 1) * P], SC[0][:, k * P:(k + 1) * P], ACT.Identity,
                                 bias=bcol[:, 1, k:k + 1], scale=scol[:, 1, k:k + 1])
                    last.then_inc(n_scaled[0], 1)
                elif kind == "logits":
                    s = item[1]
                    act.wait_ge(logitsT_psum, s + 1)
                    A(lgT[:, s * P:(s + 1) * P], PT[0][:, s * P:(s + 1) * P], ACT.Copy).then_inc(logitsT_copied, 1)
                elif kind == "proj":
                    col, n = item[1], state["proj"]
                    bank = PJ[n % 2]
                    pair = bank.rearrange("p (r t) -> p r t", r=2)
                    if col == C_KV:
                        state["proj"] += 1
                        continue
                    act.wait_ge(proj_done, n + 1)
                    if col < C_KV:
                        a = col // 256
                        A(qT[:, 2 * a:2 * a + 2, :], pair, ACT.Copy).then_inc(taken(), 1)
                    elif col < C_NG:
                        b = (col - C_KV) // 256 - 1
                        A(kT[:, b, :], bank[:, 0:T], ACT.Copy)
                        A(vS[:, :, b, :], bank[:, T:2 * T].rearrange("p (s e) -> p s e", s=TT), ACT.Copy
                          ).then_inc(taken(), 1)
                    elif col < C_V:
                        i = (col - C_QK) // 256
                        A(mlx[:, 2 * i:2 * i + 2, 3:], pair, ACT.Copy).then_inc(taken(), 1)
                    elif col < C_IF:
                        i = (col - C_V) // 256
                        for s in range(TT):
                            ins = A(mlv[:, s, 2 * i:2 * i + 2, 0:P],
                                    pair[:, s, :].rearrange("p (h e) -> p h e", h=2), ACT.Copy)
                        ins.then_inc(taken(), 1)
                    elif col < C_MG:
                        i = (col - C_O) // 256
                        A(mlo[:, :, i * 256:(i + 1) * 256], pair, ACT.Tanh, scale=0.5).then_inc(taken(), 1)
                    else:
                        i = (col - C_MG) // 256
                        A(sg[:, 2 * i:2 * i + 2, :], pair, ACT.Tanh, scale=0.5).then_inc(taken(), 1)
                elif kind == "gate_sums":
                    act.wait_ge(gate_parts, 1)
                    act.wait_ge(fold_made, 1)
                    A(gT, OB[0][:, 0:T], ACT.Copy).then_inc(gate_parts_copied, 1)
                elif kind == "gates":
                    act.wait_ge(gates_done, 1)
                    A(gn, OB[0][:, 0:48].rearrange("p (s n) -> p s n", s=TT), ACT.Tanh, scale=0.5).then_inc(gexp_done, 1)
                    act.wait_ge(ls_in, 1)
                    A(grow[:, 1, :], grow[:, 1, :], ACT.Exp, scale=-1.0).then_inc(ls_exp, 1)
                    act.wait_ge(ls_in, 2)
                    A(grow[:, 2, :], grow[:, 1, :], ACT.Ln).then_inc(ls_ln, 1)
                    act.wait_ge(nm_in, 1)
                    A(grow[:, 6, :], grow[:, 6, :], ACT.Exp, scale=-1.0).then_inc(grow_done, 1)
                elif kind == "conv_act":
                    i = item[1]
                    act.wait_ge(conv_done, i + 1)
                    A(mlx[:, 2 * i:2 * i + 2, 3:], mlc[:, 2 * i:2 * i + 2, :], ACT.Tanh, scale=0.5).then_inc(conv_exp, 1)
                elif kind == "compress" and item[1] == 1:
                    act.wait_ge(hid_done, 2)
                    for v in range(2):
                        last = A(hparts[:, v, :], PT[v][:, 0:P], ACT.Copy)
                    last.then_inc(hparts_copied, 1)
                elif kind == "cmp_fold":
                    act.wait_ge(gelu_in, 1)
                    A(htmp, htmp, ACT.Tanh, scale=GELU_A / 2).then_inc(gelu_exp, 1)
                elif kind == "cmp_scores":
                    act.wait_ge(cmp_sub, 1)
                    A(Zc, Zc, ACT.Exp, scale=NSA_SCALE).then_inc(cmp_exp, 1)
                elif kind == "head_scores":
                    h = item[1]
                    act.wait_ge(max_done, h + 1)
                    if h >= 2:
                        act.wait_ge(pt_done, h - 1)
                    for s in range(TT):
                        n = (s + 1) * P
                        for b in range(2):
                            last = A(Pb[:, h % 2, s, b, 0:n], SC[s][:, b * T:b * T + n], ACT.Exp,
                                     bias=nmx[:, h, s, b:b + 1], scale=NSA_SCALE, accum_out=psum_p[:, h, s, b:b + 1])
                    last.then_inc(exp_done, 1)
                elif kind == "head_turn":
                    h = item[1]
                    act.wait_ge(pt_done, h + 1)
                    A(PTb[:, 0, :], PT[0][:, 0:384], ACT.Copy)
                    A(PcT[0:NCMP, 0:P], PT[0][0:NCMP, 384:512], ACT.Copy).then_inc(pt_copied[0], 1)
                elif kind == "head_out":
                    h = item[1]
                    if h % 2:
                        act.wait_ge(o_done, h + 1)
                        A(oT[:, h // 2, :], OB[0][:, 0:T], ACT.Copy).then_inc(o_copied, 1)
                elif kind == "ml_scores":
                    m = item[1]
                    act.wait_ge(mls_done, m + 1)
                    if m == 0:
                        act.wait_ge(gcol_done, 1)
                    else:
                        act.wait_ge(num_done, m)
                    A(MPT[:, 0:T], SC[0][:, 0:T], ACT.Exp, scale=-1.0, bias=gcol[:, 0, 0, m:m + 1])
                    A(MPT[:, T:T + P], SC[1][:, 0:P], ACT.Exp, scale=-1.0, bias=gcol[:, 0, 1, m:m + 1]
                      ).then_inc(mle_done, 1)
                elif kind == "ml_norm":
                    act.wait_ge(var_ml, 1)
                    A(hstd, hss, ACT.Sqrt).then_inc(std_ml, 1)
                elif kind == "ml_turn":
                    act.wait_ge(mlT_turned, 1)
                    for m in range(MH):
                        A(mlT[:, m, :], SC[m // 2][:, (m % 2) * T:(m % 2 + 1) * T], ACT.Copy, scale=ngc[:, m:m + 1]
                          ).then_inc(mlT_copied, 1)
                elif kind == "router":
                    act.wait_ge(top_done, 1)
                    for s in range(TT):
                        last = A(gexp[:, s, :], top8[:, s, 0:TOPK], ACT.Exp, bias=nmax[:, s:s + 1],
                                 accum_out=gsum[:, s:s + 1])
                    last.then_inc(top_exp, 1)
                    act.wait_ge(gatesT_psum, 1)
                    A(gatesT, XB[0:NE, 0:T], ACT.Copy).then_inc(gatesT_done, 1)

            act.wait_ge(table_done, 1)

            def take_gathered(num):
                act.wait_ge(gathered, num)
                A(xg, XB[:, :], ACT.Copy).then_inc(xg_copied, 1)

            def take_turned(num):
                act.wait_ge(xg_turned, num)
                A(xgT.rearrange("p m h s -> p (m h s)"), YB[:, :], ACT.Copy).then_inc(xgT_copied, 1)

            take_gathered(1)
            take_turned(1)

            def expert_block(e, num, b, main):
                act.wait_ge(glu_min, num)
                A(sgm, glu, ACT.Sigmoid, scale=ALPHA).then_inc(sig_glu, 1)
                take_gathered(num + 1)
                act.wait_ge(gt_turned, num)
                A(GT, YB[:, 0:T], ACT.Copy).then_inc(gt_copied, 1)
                take_turned(num + 1)
                act.wait_ge(y_psum, num)
                A(ysb, YB[:, :], ACT.Copy).then_inc(y_copied, 1)

            each_block(act, expert_block)
            for s in range(TT):
                act.wait_ge(h_done, TT + 1 + s)
                A(sqj[:, s, :], xres[:, s, :], ACT.Square, accum_out=ssq[:, s:s + 1]).then_inc(ssq_done[0], 1)
            for s in range(TT):
                act.wait_ge(var_done[0], 2 + s)
                A(std[:, s:s + 1], ssq[:, s:s + 1], ACT.Sqrt).then_inc(std_done[0], 1)

        @block.vector
        def _(dve):
            chain = [0]

            def link(ins):
                chain[0] += 1
                ins.then_inc(dve_chain, 1)
                dve.wait_ge(dve_chain, chain[0])

            tt_, ts_, stt_, cp = dve.tensor_tensor, dve.tensor_scalar, dve.scalar_tensor_tensor, dve.tensor_copy
            state = {"proj": 0}

            def root(var_, root_, count, ssq_, std_, rstd_, n):
                ts_(ssq_, ssq_, 1.0 / n, EPS, ALU.mult, ALU.add).then_inc(var_, 1)
                dve.wait_ge(root_, count)
                link(dve.reciprocal(rstd_, std_))

            for item in sched:
                kind = item[0]
                if kind == "small":
                    dve.wait_ge(turned_c, 1)
                    cp(cols, SC[0][:, 0:3 * KD]).then_inc(small_copied, 1)
                    dve.wait_ge(c_exp, 1)
                    link(ts_(csig, csig, 1.0, 0.5, ALU.add, ALU.mult))
                    link(tt_(ccol, ccol, csig, ALU.mult))
                    cp(crep[:], ccol.rearrange("p (k o) -> p k o", o=1).to_broadcast([P, KD, 32])).then_inc(crep_done, 1)
                elif kind == "params":
                    dve.wait_ge(turned_small, 1)
                    link(cp(peT.rearrange("p v i -> p (v i)"), OB[1][:, 16:16 + 2 * LT]))
                    cp(convw.rearrange("p w m -> p (w m)"), OB[1][:, 64:96])
                    cp(convb, OB[1][:, 96:104])
                    ts_(ngc, OB[1][:, 104:108], 0.5, None, ALU.mult).then_inc(params_done, 1)
                    link(dve.memset(grow[:, 7, :], 0.0))
                    dve.tensor_reduce(fold[:], ident.rearrange("p (g m) -> p m g", g=4), AX, ALU.add).then_inc(fold_made, 1)
                elif kind == "norm":
                    dve.wait_ge(ssq_done[0], 1)
                    root(var_done[0], std_done[0], 1, ssq, std, rstd, D)
                    for s in range(TT):
                        ins = ts_(ntok[:, s, :], xres[:, s, :], rstd[:, s:s + 1], None, ALU.mult)
                    ins.then_inc(ntok_done, 1)
                elif kind == "second_norm":
                    s = item[1]
                    if s == 0:
                        dve.wait_ge(mix_tile0, 1)
                    else:
                        dve.wait_ge(mix_chunk, KD // 2)
                    for half in range(2):
                        ins = tt_(ntok[:, s, half * HD:(half + 1) * HD], (OB, PJ)[s][half][:, :],
                                  rg1[:, half * HD:(half + 1) * HD], ALU.mult)
                    link(ins)
                    tt_(xres[:, s, :], xres[:, s, :], ntok[:, s, :], ALU.add).then_inc(h_done, 1)
                    dve.wait_ge(ssq_done[1], s + 1)
                    ts_(ssq[:, s:s + 1], ssq[:, s:s + 1], 1.0 / D, EPS, ALU.mult, ALU.add).then_inc(var_done[1], 1)
                    dve.wait_ge(std_done[1], s + 1)
                    dve.reciprocal(rstd[:, s:s + 1], std[:, s:s + 1]).then_inc(rstd_done, 1)
                    dve.wait_ge(rstd_done, s + 1)
                    ts_(ntok[:, s, 0:HD], xres[:, s, 0:HD], rstd[:, s:s + 1], None, ALU.mult).then_inc(ntok_done, 1)
                    dve.wait_ge(h_turned, s + 1)
                    for k in range(4, KD):
                        ins = ts_(nT[:, k, s * P:(s + 1) * P], SC[1][:, (k - 4) * P:(k - 3) * P],
                                  scol[:, 1, k:k + 1], bcol[:, 1, k:k + 1], ALU.mult, ALU.add)
                    ins.then_inc(n_scaled[1], 1)
                elif kind == "mod_cols":
                    i = item[1]
                    dve.wait_ge(mod_turned, i + 1)
                    four = lambda bank, j: bank.rearrange("p (c j r) -> p j c r", c=4, j=4)[:, j:j + 2, :, 0]
                    two = lambda a: a.rearrange("p (h c) -> p h c", h=2)
                    shift, scale = ((four(SC[0], 0), four(SC[0], 2)), (four(SC[0], 2), four(SC[1], 0)))[i]
                    cp(two(bcol[:, i, :]), shift)
                    stt_(two(scol[:, i, :]), scale, 1.0, two((g1col, g2col)[i]), ALU.add, ALU.mult).then_inc(cols_done, 1)
                    if i == 0:
                        dve.wait_ge(cols_done, 1)
                        for q in (1, 3):
                            dve.wait_ge(nT_copied[1], q // 2 + 1)
                            for k in (2 * q, 2 * q + 1):
                                ins = ts_(nT[:, k, :], nT[:, k, :], scol[:, 0, k:k + 1], bcol[:, 0, k:k + 1], ALU.mult, ALU.add)
                        ins.then_inc(n_scaled[1], 1)
                elif kind == "gate_evac":
                    dve.wait_ge(rows_done, 1)
                    for half in range(2):
                        ins = ts_(rg1[:, half * HD:(half + 1) * HD], PT[half][:, :], 1.0, 0.5, ALU.add, ALU.mult)
                    ins.then_inc(rows_used, 1)
                    dve.wait_ge(rows_used, 1)
                elif kind == "mod":
                    p = item[1]
                    dve.wait_ge(ada_chunk, KD * (p + 1))
                    if p == 0:
                        dve.wait_ge(adab_in, 16 * 4)
                    tt_(modrow[:, p, :], modrow[:, p, :], OB[min(p, 1)][:, :], ALU.add).then_inc(mod_done, 1)
                elif kind == "turn":
                    for q in (1, 3):
                        dve.wait_ge(n_turned, q + 1)
                        cp(nT[:, 2 * q:2 * q + 2, :], PJ[1].rearrange("p (a t) -> p a t", a=2)).then_inc(nT_copied[1], 1)
                elif kind == "proj":
                    n = state["proj"]
                    state["proj"] += 1
                    if item[1] == C_KV:
                        dve.wait_ge(proj_done, n + 1)
                        for v in range(2):
                            for g in range(2):
                                for a in range(2):
                                    src = PJ[n % 2][64 * g:64 * g + 64, v * T:(v + 1) * T]
                                    out_ = kpe[64 * a:64 * a + 64, v, :, g * NCMP:(g + 1) * NCMP]
                                    pos_ = peT[64 * a:64 * a + 64, v, :]
                                    for hb in range(2):
                                        i0 = hb * LT // 2
                                        src_ = src[:, hb * STRIDE:hb * STRIDE + NCMP * STRIDE].rearrange(
                                            "p (n i a) -> p a i n", i=LT // 2, a=2)[:, a]
                                        ins = tt_(out_[:, i0:i0 + LT // 2, :], src_,
                                                  pos_[:, i0:i0 + LT // 2].rearrange("p (i o) -> p i o", o=1)
                                                  .to_broadcast([64, LT // 2, NCMP]), ALU.add)
                        ins.then_inc(proj_taken[n % 2], 1)
                elif kind == "gates":
                    dve.wait_ge(gates_done, 1)
                    dve.wait_ge(gate_b_in, 16)
                    link(ts_(grow[:, 0, :], SC[0][0:MH, 64:64 + T], gb[0:MH, 1:2], None, ALU.add))
                    stt_(grow[:, 1, :], grow[:, 0, :], -1.0, grow[:, 0, :], ALU.mult, ALU.max).then_inc(ls_in, 1)
                    dve.wait_ge(ls_exp, 1)
                    ts_(grow[:, 1, :], grow[:, 1, :], 1.0, None, ALU.add).then_inc(ls_in, 1)
                    dve.wait_ge(ls_ln, 1)
                    link(stt_(grow[:, 0, :], grow[:, 0, :], 0.0, grow[:, 2, :], ALU.min, ALU.subtract))
                    link(dve.tensor_tensor_scan(grow[:, 3, :], grow[:, 0, :], grow[:, 7, :], 0.0, ALU.add, ALU.add))
                    dve.wait_ge(gexp_done, 1)
                    link(stt_(grow[:, 5, :], OB[0][0:MH, 64:64 + T], gb[0:MH, 0:1], grow[:, 3, :], ALU.add, ALU.subtract))
                    link(dve.tensor_tensor_scan(grow[:, 4, :], grow[:, 5, :], grow[:, 5, :], 0.0, ALU.max, ALU.max))
                    tt_(grow[:, 6, :], grow[:, 3, :], grow[:, 4, :], ALU.add).then_inc(nm_in, 1)
                    link(ts_(gn, gn, 1.0, 0.5, ALU.add, ALU.mult))
                elif kind == "gate_cols":
                    dve.wait_ge(gcol_turned, 1)
                    cp(gcol.rearrange("p a s h -> p (a s h)"), SC[1][:, 0:16]).then_inc(gcol_done, 1)
                elif kind == "conv":
                    i = item[1]
                    if i == 0:
                        dve.wait_ge(masks, MASKS)
                    n = state["proj"] - 1
                    dve.wait_ge(proj_taken[n % 2], n // 2 + 1)
                    for w in (3, 2, 1, 0):
                        for m in (2 * i, 2 * i + 1):
                            if w == 3:
                                ins = ts_(mlc[:, m, :], mlx[:, m, 3:3 + T], convw[:, 3, m:m + 1], convb[:, m:m + 1],
                                          ALU.mult, ALU.add)
                            else:
                                ins = stt_(mlc[:, m, :], mlx[:, m, w:w + T], convw[:, w, m:m + 1], mlc[:, m, :],
                                           ALU.mult, ALU.add)
                        if w:
                            link(ins)
                    ins.then_inc(conv_done, 1)
                elif kind == "conv_act":
                    i = item[1]
                    dve.wait_ge(conv_exp, i + 1)
                    ex, cc = mlx[:, 2 * i:2 * i + 2, 3:], mlc[:, 2 * i:2 * i + 2, :]
                    stt_(cc, ex, 1.0, cc, ALU.add, ALU.mult).then_inc(conv_act, 1)
                elif kind == "cmp_fold":
                    dve.wait_ge(cw2_in, 16 * 2)
                    cp(cw2d.rearrange("p (a e) -> p a e", a=2),
                       cw2[:, 0, :].rearrange("p (a e) -> p a e", a=1).to_broadcast([P, 2, DH]))
                    dve.wait_ge(hid_folded, 1)
                    for v in range(2):
                        ins = cp(hid[:, v, :], PT[v][:, P:P + NG])
                    link(ins)
                    link(tt_(htmp, hid, hid, ALU.mult))
                    link(ts_(htmp, htmp, GELU_B, 1.0, ALU.mult, ALU.add))
                    tt_(htmp, htmp, hid, ALU.mult).then_inc(gelu_in, 1)
                    dve.wait_ge(gelu_exp, 1)
                    link(ts_(htmp, htmp, 1.0, 0.5, ALU.add, ALU.mult))
                    tt_(hid, hid, htmp, ALU.mult).then_inc(hid_act, 1)
                elif kind == "cmp_keys":
                    dve.wait_ge(cmp_kv, 1)
                    cp(kcT, PT[0][:, 64:64 + NG])
                    cp(vc[0:NCMP, :, :], PT[0][0:NCMP, 128:256].rearrange("p (g e) -> p g e", g=2)).then_inc(cmp_kv_sb, 1)
                elif kind == "cmp_scores":
                    dve.wait_ge(cmp_score, 1)
                    for g in range(2):
                        sc_ = (OB[0], SC[0])[g][:, 0:TT * NR * NCMP].rearrange("p (s h n) -> p s h n", s=TT, h=NR)
                        ins = tt_(Zc[:, :, g * NR:(g + 1) * NR, :], sc_, cneg[:, :, 0:NR, :], ALU.add)
                    link(ins)
                    link(dve.tensor_reduce(cmx, Zc, AX, ALU.max))
                    bc = lambda a: a.rearrange("p s (h o) -> p s h o", o=1).to_broadcast([P, TT, NH, NCMP])
                    tt_(Zc, Zc, bc(cmx), ALU.subtract).then_inc(cmp_sub, 1)
                    dve.wait_ge(cmp_exp, 1)
                    link(dve.tensor_reduce(csum, Zc, AX, ALU.add))
                    link(dve.reciprocal(csum, csum))
                    link(tt_(csum, csum, gn[:, :, 0:NH], ALU.mult))
                    link(tt_(Zc, Zc, c01, ALU.mult))
                    tt_(Pc, Zc, bc(csum), ALU.mult).then_inc(cmp_p, 1)
                elif kind == "head_scores":
                    h = item[1]
                    dve.wait_ge(score_done, h + 1)
                    for s in range(TT):
                        n = (s + 1) * P
                        ins = dve.tensor_reduce(mx[:, h, s, :], SC[s].rearrange("p (b t) -> p b t", b=2)[:, :, 0:n],
                                                AX, ALU.max)
                    link(ins)
                    ts_(nmx[:, h], mx[:, h], -NSA_SCALE, None, ALU.mult).then_inc(max_done, 1)
                    dve.wait_ge(exp_done, h + 1)
                    link(dve.reciprocal(rsc[:, h], psum_p[:, h]))
                    link(tt_(rsc[:, h], rsc[:, h], gn[:, :, NH + h:3 * NH:NH], ALU.mult))
                    for s in range(TT):
                        n = (s + 1) * P
                        pp = Pb[:, h % 2, s, :, 0:n]
                        ins = tt_(pp, pp, rsc[:, h, s, :].rearrange("p (b o) -> p b o", o=1).to_broadcast([P, 2, n]), ALU.mult)
                    ins.then_inc(probs_done, 1)
                elif kind == "head_turn":
                    h = item[1]
                    dve.wait_ge(pt_done, h + 1)
                    cp(PTb[:, 1, :], PT[1][:, 0:384])
                    cp(PcT[0:NCMP, P:2 * P], PT[1][0:NCMP, 384:512]).then_inc(pt_copied[1], 1)
                elif kind == "ml_scores":
                    m = item[1]
                    dve.wait_ge(mle_done, m + 1)
                    stt_(MPT[:, 0:T], SC[0][:, T:2 * T], ML_SCALE / 4, MPT[:, 0:T], ALU.mult, ALU.mult)
                    stt_(MPT[:, T:T + P], SC[1][:, T:T + P], ML_SCALE / 4, MPT[:, T:T + P], ALU.mult, ALU.mult
                         ).then_inc(mpt_done, 1)
                elif kind == "ml_out":
                    m = item[1]
                    dve.wait_ge(num_done, m + 1)
                    nd = PT[0][:, 0:258].rearrange("p (s e) -> p s e", s=TT)
                    d_ = den[:, m, :].rearrange("p (s o) -> p s o", o=1)
                    link(cp(d_, nd[:, :, 128:129]))
                    link(stt_(d_, d_, -1.0, d_, ALU.mult, ALU.max))
                    link(tt_(d_, d_, gcol[:, 1, :, m:m + 1], ALU.max))
                    link(dve.reciprocal(d_, d_))
                    tt_(hml[:, :, m * P:(m + 1) * P], nd[:, :, 0:P], d_.to_broadcast([P, TT, P]), ALU.mult
                        ).then_inc(hml_done, 1)
                elif kind == "ml_norm":
                    dve.wait_ge(hml_done, MH)
                    link(tt_(hsq, hml, hml, ALU.mult))
                    link(dve.tensor_reduce(hss, hsq.rearrange("p s (h e) -> p (s h) e", h=MH), AX, ALU.add))
                    root(var_ml, std_ml, 1, hss, hstd, hr, P)
                    h4 = hml.rearrange("p s (h e) -> p (s h) e", h=MH)
                    link(tt_(h4, h4, hr.rearrange("p (n o) -> p n o", o=1).to_broadcast([P, TT * MH, P]), ALU.mult))
                    dve.wait_ge(proj_taken[0], (n_proj + 1) // 2)
                    dve.wait_ge(proj_taken[1], n_proj // 2)
                    stt_(hml, mlo, 1.0, hml, ALU.add, ALU.mult).then_inc(hml_norm, 1)
                elif kind == "up":
                    a = item[1]
                    for q in range(4):
                        dve.wait_ge(up_done, 4 * a + q + 1)
                        pair = PJ[q % 2].rearrange("p (i t) -> p i t", i=2)
                        dst = merged[:, 2 * q:2 * q + 2, :]
                        if a == 0:
                            stt_(dst, sg[:, 2 * q:2 * q + 2, :], 1.0, pair, ALU.add, ALU.mult).then_inc(up_taken, 1)
                        else:
                            tmp = mtmp.rearrange("p (i t) -> p i t", i=2)
                            ins = stt_(tmp, sg[:, 8 + 2 * q:8 + 2 * q + 2, :], 1.0, pair, ALU.add, ALU.mult)
                            ins.then_inc(up_taken, 1)
                            dve.wait_ge(up_taken, 4 + q + 1)
                            ins = tt_(dst, dst, tmp, ALU.add)
                            if q < 3:
                                link(ins)
                    if a:
                        ins.then_inc(merged_done, 1)
                elif kind == "router":
                    dve.wait_ge(router_done, 1)
                    link(dve.tensor_reduce(logit, PT[1][:, 0:TT * P].rearrange("p (s g e) -> p s e g", s=TT, g=4), AX, ALU.add))
                    dve.wait_ge(moe_in, 16 * 3)
                    link(tt_(logit, logit, rbias.rearrange("p (a e) -> p a e", a=1).to_broadcast([P, TT, NE]), ALU.add))
                    for s in range(TT):
                        ins = dve.max(top8[:, s, :], logit[:, s, :])
                    link(ins)
                    ts_(nmax, top8[:, :, 0], -1.0, None, ALU.mult).then_inc(top_done, 1)
                    for s in range(TT):
                        ins = dve.max_index(idx8[:, s, :], top8[:, s, :], logit[:, s, :])
                    link(ins)
                    link(cp(idxf[:], idx8[:]))
                    dve.wait_ge(iota_made, 1)
                    every = [P, TT, TOPK, NE]
                    link(tt_(chosen, iota_f[:, 0, 0, 0:NE].rearrange("p (a b e) -> p a b e", a=1, b=1).to_broadcast(every),
                             idxf[:, :, 0:TOPK].rearrange("p s (j o) -> p s j o", o=1).to_broadcast(every), ALU.is_equal))
                    by_expert = chosen.rearrange("p s j e -> p s e j")
                    dve.tensor_reduce(memb, by_expert, AX, ALU.add).then_inc(memb_done, 1)
                    dve.wait_ge(top_exp, 1)
                    link(dve.reciprocal(grs, gsum))
                    link(tt_(gexp, gexp, grs.rearrange("p (s o) -> p s o", o=1).to_broadcast([P, TT, TOPK]), ALU.mult))
                    dve.wait_ge(memb_done, 1)
                    link(tt_(chosen, chosen, gexp.rearrange("p s (j o) -> p s j o", o=1).to_broadcast(every), ALU.mult))
                    cp(sel_e, ident[0:NE, 0:1].to_broadcast([NE, SLOTS]))
                    dve.tensor_reduce(gate, by_expert, AX, ALU.add).then_inc(gate_made, 1)
                    dve.wait_ge(rank_psum, 1)
                    link(dve.memset(rank, -1.0))
                    rk = rank[:, :, 0:NE]
                    link(stt_(rk, PT[0][:, 0:2 * NE].rearrange("p (s e) -> p s e", s=TT), 1.0, memb, ALU.add, ALU.mult))
                    link(ts_(rk, rk, -1.0, None, ALU.add))
                    cnt, nblk, upto, zero = (cntf[0:1, a, :] for a in range(4))
                    link(cp(cnt, PT[0][0:1, 64:64 + NE]))
                    dve.memset(zero, 0.0)
                    link(ts_(nblk, cnt, SLOTS + 0.5, 1.0, ALU.is_gt, ALU.add))
                    for b in range(2, NBLK):
                        link(stt_(nblk, cnt, SLOTS * b + 0.5, nblk, ALU.is_gt, ALU.add))
                    link(dve.tensor_tensor_scan(upto, nblk, zero, 0.0, ALU.add, ALU.add))
                    cp(cnt_t[:], cnt)
                    dve.memset(blk_t[0:1, 0:1], 0)
                    link(dve.memset(next_t[:], 0))
                    for b in range(NBLK - 1):
                        ts_(next_t[0:1, b, 0:NE], cnt, SLOTS * (b + 1) + 0.5, float(b + 1), ALU.is_gt, ALU.mult)
                    cp(blk_t[0:1, 1:NE + 1], upto).then_inc(table_done, 1)

            dve.wait_ge(table_done, 1)

            def make_hot(e_, b_, first=False):
                hot = iota_f[:, bass.ds(b_, 1), 0, :].rearrange("p a n -> p (a n)")
                for s in range(TT):
                    ins = ts_(onehot[:, s, :], hot, rank[:, s, bass.ds(e_, 1)], None, ALU.is_equal)
                if first:
                    ins.then_inc(hot_done, 1)
                else:
                    cp(sel_e, ident[0:NE, bass.ds(e_, 1)].to_broadcast([NE, SLOTS])).then_inc(hot_done, 1)

            make_hot(0, dve.value_load(next_t[0:1, 0, 0:1], min_val=0, max_val=NBLK - 1), first=True)
            dve.memset(ysb, 0.0).then_inc(y_copied, 1)
            dve.memset(GT, 0.0).then_inc(gt_copied, 1)

            def scale_gathered(num):
                dve.wait_ge(xgT_copied, num)
                col = lambda a: a[:, 1, :].rearrange("p (h m o) -> p m h o", h=2, o=1).to_broadcast([P, 4, 2, SLOTS])
                tt_(xgT, xgT, col(scol), ALU.mult).then_inc(xg_scaled, 1)
                dve.wait_ge(xg_scaled, num)
                tt_(xgT, xgT, col(bcol), ALU.add).then_inc(xgT_scaled, 1)

            scale_gathered(1)
            dve.wait_ge(rows_done, 2)
            for half in range(2):
                ins = ts_(rg2[:, half * HD:(half + 1) * HD], OB[half][:, :], 1.0, None, ALU.add)
            ins.then_inc(rows_used, 1)

            def expert_block(e, num, b, main):
                after = e + 1 if main else e
                b_after = dve.value_load(next_t[0:1, b, bass.ds(after, 1)], min_val=0, max_val=NBLK - 1)
                dve.wait_ge(biased, num)
                make_hot(after, b_after)
                hot = iota_f[:, b, :, :].rearrange("p a n -> p (a n)")
                for s in range(TT):
                    ins = ts_(onegate[:, s, :], hot, rank[:, s, bass.ds(e, 1)], gate[:, s, bass.ds(e, 1)],
                              ALU.is_equal, ALU.mult)
                ins.then_inc(onegate_done, 1)
                dve.wait_ge(h_psum, num)
                ts_(glu, HG[:, :], LIMIT, None, ALU.min).then_inc(glu_min, 1)
                ts_(lin, HL[:, :], LIMIT, -LIMIT, ALU.min, ALU.max)
                dve.wait_ge(sig_glu, num)
                tt_(glu, glu, sgm, ALU.mult).then_inc(glu_gated, 1)
                dve.wait_ge(glu_gated, num)
                stt_(act_t, lin, 1.0, glu, ALU.add, ALU.mult).then_inc(act_made, 1)
                dve.wait_ge(act_turned, num)
                cp(actT.rearrange("p m h s -> p (m h s)"), XB[:, :]).then_inc(actT_copied, 1)
                scale_gathered(num + 1)

            each_block(dve, expert_block)
            dve.wait_ge(rows_used, 2)
            for s in range(TT):
                dve.wait_ge(added, s + 1)
                for half in range(2):
                    ins = tt_(otmp[:, s, half * HD:(half + 1) * HD], ACC[s][half][:, :],
                              rg2[:, half * HD:(half + 1) * HD], ALU.mult)
                link(ins)
                tt_(xres[:, s, :], xres[:, s, :], otmp[:, s, :], ALU.add).then_inc(h_done, 1)
            dve.wait_ge(rfin_in, 16)
            for s in range(TT):
                dve.wait_ge(ssq_done[0], 2 + s)
                one = slice(s, s + 1)
                root(var_done[0], std_done[0], 2 + s, ssq[:, one], std[:, one], rstd[:, one], D)
                stt_(otmp[:, s, :], xres[:, s, :], rstd[:, one], rfin, ALU.mult, ALU.mult).then_inc(final_done, 1)


_INS = ['x', 'c', 'ada_w', 'ada_b', 'norm1_g', 'w_in', 'nsa_pe_k', 'nsa_pe_v', 'nsa_cmp_w1_k', 'nsa_cmp_w2_k',
        'nsa_cmp_w1_v', 'nsa_cmp_w2_v', 'ml_conv_w', 'ml_conv_b', 'ml_gate_b', 'ml_norm_g', 'w_up_nsa', 'w_up_ml',
        'w_out', 'norm2_g', 'router_w', 'router_b', 'exp_w1', 'exp_b1', 'exp_w2', 'exp_b2', 'final_g']


def kernel(**inputs):
    import numpy as _np
    import concourse.bacc as _bacc
    from concourse import mybir as _mybir
    from concourse.bass_utils import run_bass_kernel_spmd as _run

    nc = _bacc.Bacc("TRN2", target_bir_lowering=False, num_devices=1)
    arrays, args = {}, []
    for name in _INS:
        a = _np.ascontiguousarray(inputs[name])
        if name not in ('c', 'final_g'):
            a = a[0]
        arrays[f"in_{name}_dram"] = a
        args.append(nc.dram_tensor(f"in_{name}_dram", a.shape, _mybir.dt.from_np(a.dtype), kind="ExternalInput").ap())
    shape = inputs['x'].shape
    args.append(nc.dram_tensor("out_0_dram", shape[1:], _mybir.dt.float32, kind="ExternalOutput").ap())
    hybrid_block(nc, *args)
    r = _run(nc, [arrays], core_ids=[0])
    return r.results[0]["out_0_dram"].reshape(shape)
```
